# Optimizing a Trainium2 kernel written in Bass

```python
import math, functools
import jax, jax.numpy as jnp
from jax import lax
import numpy as np

D_MODEL = 2048
BATCH = 1
SEQ = 512
DEPTH = 1
DEC_BATCH = 8
DEC_SEQ = 8
PAST_LEN = 2048
PAGE_SIZE = 128

ATT_WIDTH = D_MODEL // 2
SSM_WIDTH = D_MODEL - ATT_WIDTH
HEAD_DIM = 128
N_ATT_HEADS = ATT_WIDTH // HEAD_DIM
SSM_GROUP = 16
N_SSM_GROUPS = SSM_WIDTH // SSM_GROUP
SSM_STATE = 64
D_FF = 4 * D_MODEL
Q_BLOCK = 128
ALPHA = (2 * DEPTH) ** 0.25
BETA = (8 * DEPTH) ** -0.25
LN_EPS = 1e-5
N_MOD = 6
IN_COLS = 3 * ATT_WIDTH + N_ATT_HEADS + SSM_WIDTH
SCALE = HEAD_DIM ** -0.5
FORGET_BIAS_LO = 2.0
FORGET_BIAS_HI = 10.0

kernel_name = "fox_s5_parallel_heads_deepnorm_adaln_step"

def _layer_norm(x, g=None, b=None):
    xf = x.astype(jnp.float32)
    mu = jnp.mean(xf, axis=-1, keepdims=True)
    var = jnp.mean(jnp.square(xf - mu), axis=-1, keepdims=True)
    y = (xf - mu) * lax.rsqrt(var + LN_EPS)
    if g is not None:
        y = y * g.astype(jnp.float32) + b.astype(jnp.float32)
    return y.astype(x.dtype)

def _attend_prompt(q, k, v, logf):
    bsz, s_len = q.shape[:2]
    n_blk = s_len // Q_BLOCK
    f_cum = jnp.transpose(lax.cumsum(logf, axis=1), (0, 2, 1))
    q_blk = jnp.transpose(q.reshape(bsz, n_blk, Q_BLOCK, N_ATT_HEADS, HEAD_DIM), (1, 0, 2, 3, 4))
    f_blk = jnp.transpose(f_cum.reshape(bsz, N_ATT_HEADS, n_blk, Q_BLOCK), (2, 0, 1, 3))
    k_pos = jnp.arange(s_len)

    def block(args):
        qi, fi, i = args
        s = (jnp.einsum('bqhd,bkhd->bhqk', qi, k).astype(jnp.float32) * SCALE
             + fi[..., :, None] - f_cum[:, :, None, :])
        q_pos = i * Q_BLOCK + jnp.arange(Q_BLOCK)
        s = jnp.where(k_pos[None, :] <= q_pos[:, None], s, -jnp.inf)
        p = jax.nn.softmax(s, axis=-1).astype(v.dtype)
        return jnp.einsum('bhqk,bkhd->bqhd', p, v)

    out = lax.map(block, (q_blk, f_blk, jnp.arange(n_blk)))
    return jnp.transpose(out, (1, 0, 2, 3, 4)).reshape(bsz, s_len, ATT_WIDTH)

def _attend_sample(q, k, v, logf, cache_k, cache_v, cache_logf, page_table):
    nb, n_q = q.shape[:2]
    k_past = cache_k[page_table].reshape(nb, -1, N_ATT_HEADS, HEAD_DIM)
    v_past = cache_v[page_table].reshape(nb, -1, N_ATT_HEADS, HEAD_DIM)
    lf_past = cache_logf[page_table].reshape(nb, -1, N_ATT_HEADS).astype(jnp.float32)
    past = k_past.shape[1]
    f_new = jnp.transpose(lax.cumsum(logf, axis=1), (0, 2, 1))
    decay_past = jnp.transpose(lax.cumsum(lf_past, axis=1, reverse=True) - lf_past, (0, 2, 1))
    s_past = (jnp.einsum('bqhd,bkhd->bhqk', q, k_past).astype(jnp.float32) * SCALE
              + decay_past[:, :, None, :] + f_new[:, :, :, None])
    s_new = (jnp.einsum('bqhd,bkhd->bhqk', q, k).astype(jnp.float32) * SCALE
             + f_new[:, :, :, None] - f_new[:, :, None, :])
    causal = jnp.arange(n_q)[None, :] <= jnp.arange(n_q)[:, None]
    s_new = jnp.where(causal, s_new, -jnp.inf)
    p = jax.nn.softmax(jnp.concatenate([s_past, s_new], axis=-1), axis=-1).astype(v.dtype)
    out = (jnp.einsum('bhqk,bkhd->bqhd', p[..., :past], v_past)
           + jnp.einsum('bhqk,bkhd->bqhd', p[..., past:], v))
    return out.reshape(nb, n_q, ATT_WIDTH)

def _s5(u, h0, a_re, a_im, log_dt, b_re, b_im, c_re, c_im, d_skip, w_glu, b_glu):
    f32 = jnp.float32
    bsz, l_len = u.shape[:2]
    u = u.astype(f32).reshape(bsz, l_len, N_SSM_GROUPS, SSM_GROUP)
    a_re, a_im = a_re.astype(f32), a_im.astype(f32)
    dt = jnp.exp(log_dt.astype(f32))[:, None]
    mag = jnp.exp(a_re * dt)
    lam_re, lam_im = mag * jnp.cos(a_im * dt), mag * jnp.sin(a_im * dt)
    den = jnp.square(a_re) + jnp.square(a_im)
    n_re = lam_re - 1.0
    k_re = (n_re * a_re + lam_im * a_im) / den
    k_im = (lam_im * a_re - n_re * a_im) / den
    b_re, b_im = b_re.astype(f32), b_im.astype(f32)
    bb_re = k_re[..., None] * b_re - k_im[..., None] * b_im
    bb_im = k_re[..., None] * b_im + k_im[..., None] * b_re
    bu_re = jnp.einsum('blgc,gpc->blgp', u, bb_re)
    bu_im = jnp.einsum('blgc,gpc->blgp', u, bb_im)
    ar = jnp.broadcast_to(lam_re, bu_re.shape)
    ai = jnp.broadcast_to(lam_im, bu_re.shape)

    def combine(e1, e2):
        a1r, a1i, b1r, b1i = e1
        a2r, a2i, b2r, b2i = e2
        return (a1r * a2r - a1i * a2i, a1r * a2i + a1i * a2r,
                a2r * b1r - a2i * b1i + b2r, a2r * b1i + a2i * b1r + b2i)

    _, _, h_re, h_im = lax.associative_scan(combine, (ar, ai, bu_re, bu_im), axis=1)
    if h0 is not None:
        h0_re, h0_im = h0[0].astype(f32)[:, None], h0[1].astype(f32)[:, None]
        steps = jnp.arange(1, l_len + 1, dtype=f32)[:, None, None]
        pm = jnp.exp(a_re * dt * steps)
        p_re, p_im = pm * jnp.cos(a_im * dt * steps), pm * jnp.sin(a_im * dt * steps)
        h_re = h_re + p_re * h0_re - p_im * h0_im
        h_im = h_im + p_re * h0_im + p_im * h0_re
    y = (jnp.einsum('gcp,blgp->blgc', c_re.astype(f32), h_re)
         - jnp.einsum('gcp,blgp->blgc', c_im.astype(f32), h_im)
         + d_skip.astype(f32) * u)
    z = jax.nn.gelu(y)
    zz = jnp.einsum('blgc,gce->blge', z, w_glu.astype(f32)) + b_glu.astype(f32)
    out = zz[..., :SSM_GROUP] * jax.nn.sigmoid(zz[..., SSM_GROUP:])
    return out.reshape(bsz, l_len, SSM_WIDTH), h_re[:, -1], h_im[:, -1]

def _trunk_layer(x, c, attend, h0, w_ada, b_ada, w_in, b_f, w_o, a_re, a_im, log_dt,
                 b_re, b_im, c_re, c_im, d_skip, w_glu, b_glu, ln1_g, ln1_b,
                 w_up, w_down, ln2_g, ln2_b):
    bsz, l_len, _ = x.shape
    mod = (jax.nn.silu(c) @ w_ada + b_ada).reshape(bsz, N_MOD, 1, D_MODEL)
    shift1, scale1, gate1, shift2, scale2, gate2 = (mod[:, i] for i in range(N_MOD))
    h = _layer_norm(x) * (1 + scale1) + shift1
    proj = h @ w_in
    cuts = [ATT_WIDTH, 2 * ATT_WIDTH, 3 * ATT_WIDTH, 3 * ATT_WIDTH + N_ATT_HEADS]
    q, k, v, f_logit, u = jnp.split(proj, cuts, axis=-1)
    q = q.reshape(bsz, l_len, N_ATT_HEADS, HEAD_DIM)
    k = k.reshape(bsz, l_len, N_ATT_HEADS, HEAD_DIM)
    v = v.reshape(bsz, l_len, N_ATT_HEADS, HEAD_DIM)
    logf = jax.nn.log_sigmoid(f_logit.astype(jnp.float32) + b_f.astype(jnp.float32))
    att = attend(q, k, v, logf)
    ssm, h_re, h_im = _s5(u, h0, a_re, a_im, log_dt, b_re, b_im, c_re, c_im, d_skip, w_glu, b_glu)
    mix = jnp.concatenate([att, ssm.astype(x.dtype)], axis=-1) @ w_o
    x = _layer_norm(ALPHA * x + (1 + gate1) * mix, ln1_g, ln1_b)
    h2 = _layer_norm(x) * (1 + scale2) + shift2
    m = jnp.square(jax.nn.relu(h2 @ w_up)) @ w_down
    x = _layer_norm(ALPHA * x + (1 + gate2) * m, ln2_g, ln2_b)
    return x, k, v, logf.astype(x.dtype), h_re, h_im

def setup_inputs(seed: int = 0) -> dict:
    key = jax.random.key(seed)
    ks = iter(jax.random.split(key, 40))
    nrm = lambda shape, s=1.0: jax.random.normal(next(ks), shape, jnp.float32) * s
    n_pages = PAST_LEN // PAGE_SIZE
    n_used = DEC_BATCH * n_pages
    n_pool = n_used + max(1, n_used // 4)
    page_table = jax.random.permutation(next(ks), n_pool)[:n_used].reshape(DEC_BATCH, n_pages).astype(jnp.int32)
    L = DEPTH
    head_bias = jnp.linspace(FORGET_BIAS_LO, FORGET_BIAS_HI, N_ATT_HEADS, dtype=jnp.float32)
    return {
        "x_prompt": nrm((BATCH, SEQ, D_MODEL)),
        "x_sample": nrm((DEC_BATCH, DEC_SEQ, D_MODEL)),
        "c_prompt": nrm((BATCH, D_MODEL)),
        "c_sample": nrm((DEC_BATCH, D_MODEL)),
        "cache_k": nrm((L, n_pool, PAGE_SIZE, N_ATT_HEADS, HEAD_DIM)),
        "cache_v": nrm((L, n_pool, PAGE_SIZE, N_ATT_HEADS, HEAD_DIM)),
        "cache_logf": jax.nn.log_sigmoid(head_bias + nrm((L, n_pool, PAGE_SIZE, N_ATT_HEADS), 0.5)),
        "state_ssm_re": nrm((L, DEC_BATCH, N_SSM_GROUPS, SSM_STATE), 0.1),
        "state_ssm_im": nrm((L, DEC_BATCH, N_SSM_GROUPS, SSM_STATE), 0.1),
        "page_table": page_table,
        "w_ada": nrm((L, D_MODEL, N_MOD * D_MODEL), 0.5 * D_MODEL ** -0.5),
        "b_ada": nrm((L, N_MOD * D_MODEL), 0.02),
        "w_in": nrm((L, D_MODEL, IN_COLS), D_MODEL ** -0.5),
        "b_f": head_bias + nrm((L, N_ATT_HEADS), 0.5),
        "w_o": nrm((L, D_MODEL, D_MODEL), BETA * D_MODEL ** -0.5),
        "a_re": -0.5 * jnp.exp(nrm((L, N_SSM_GROUPS, SSM_STATE), 0.05)),
        "a_im": jnp.pi * jnp.arange(SSM_STATE, dtype=jnp.float32) + nrm((L, N_SSM_GROUPS, SSM_STATE), 0.01),
        "log_dt": jax.random.uniform(next(ks), (L, N_SSM_GROUPS), jnp.float32, math.log(1e-3), math.log(1e-1)),
        "b_re": nrm((L, N_SSM_GROUPS, SSM_STATE, SSM_GROUP), (2 * SSM_GROUP) ** -0.5),
        "b_im": nrm((L, N_SSM_GROUPS, SSM_STATE, SSM_GROUP), (2 * SSM_GROUP) ** -0.5),
        "c_re": nrm((L, N_SSM_GROUPS, SSM_GROUP, SSM_STATE), (2 * SSM_STATE) ** -0.5),
        "c_im": nrm((L, N_SSM_GROUPS, SSM_GROUP, SSM_STATE), (2 * SSM_STATE) ** -0.5),
        "d_skip": nrm((L, N_SSM_GROUPS, SSM_GROUP)),
        "w_glu": nrm((L, N_SSM_GROUPS, SSM_GROUP, 2 * SSM_GROUP), SSM_GROUP ** -0.5),
        "b_glu": nrm((L, N_SSM_GROUPS, 2 * SSM_GROUP), 0.02),
        "ln1_g": 1.0 + nrm((L, D_MODEL), 0.02),
        "ln1_b": nrm((L, D_MODEL), 0.02),
        "w_up": nrm((L, D_MODEL, D_FF), D_MODEL ** -0.5),
        "w_down": nrm((L, D_FF, D_MODEL), BETA * D_FF ** -0.5),
        "ln2_g": 1.0 + nrm((L, D_MODEL), 0.02),
        "ln2_b": nrm((L, D_MODEL), 0.02),
    }

def reference(x_prompt, x_sample, c_prompt, c_sample, cache_k, cache_v, cache_logf,
              state_ssm_re, state_ssm_im, page_table, w_ada, b_ada, w_in, b_f, w_o,
              a_re, a_im, log_dt, b_re, b_im, c_re, c_im, d_skip, w_glu, b_glu,
              ln1_g, ln1_b, w_up, w_down, ln2_g, ln2_b):
    yp, ys = x_prompt, x_sample
    kp_l, vp_l, fp_l, hpr_l, hpi_l = [], [], [], [], []
    ks_l, vs_l, fs_l, hsr_l, hsi_l = [], [], [], [], []
    for l in range(DEPTH):
        weights = (w_ada[l], b_ada[l], w_in[l], b_f[l], w_o[l], a_re[l], a_im[l], log_dt[l],
                   b_re[l], b_im[l], c_re[l], c_im[l], d_skip[l], w_glu[l], b_glu[l],
                   ln1_g[l], ln1_b[l], w_up[l], w_down[l], ln2_g[l], ln2_b[l])
        yp, kp, vp, fp, hpr, hpi = _trunk_layer(yp, c_prompt, _attend_prompt, None, *weights)
        attend_s = functools.partial(_attend_sample, cache_k=cache_k[l], cache_v=cache_v[l],
                                     cache_logf=cache_logf[l], page_table=page_table)
        ys, kss, vss, fss, hsr, hsi = _trunk_layer(ys, c_sample, attend_s,
                                                   (state_ssm_re[l], state_ssm_im[l]), *weights)
        kp_l.append(kp); vp_l.append(vp); fp_l.append(fp); hpr_l.append(hpr); hpi_l.append(hpi)
        ks_l.append(kss); vs_l.append(vss); fs_l.append(fss); hsr_l.append(hsr); hsi_l.append(hsi)
    return (yp, ys,
            jnp.stack(kp_l), jnp.stack(vp_l), jnp.stack(fp_l), jnp.stack(hpr_l), jnp.stack(hpi_l),
            jnp.stack(ks_l), jnp.stack(vs_l), jnp.stack(fs_l), jnp.stack(hsr_l), jnp.stack(hsi_l))


_drawn_inputs = setup_inputs


def setup_inputs(seed=0):
    import zlib

    import numpy as np

    out = dict(_drawn_inputs(seed))
    spreads = {}
    factors = {'c_re': 5.986, 'c_im': 5.912, 'b_glu': 8.0, 'ln1_b': 2.801, 'ln2_g': 2.846, 'ln2_b': 2.769}
    for name, (base, spread) in spreads.items():
        noise = np.random.default_rng([zlib.crc32(name.encode()), seed]).standard_normal(out[name].shape)
        drawn = base * np.exp(spread * noise) if base else spread * noise
        out[name] = __import__('jax').numpy.asarray(drawn.astype(out[name].dtype))
    for name, factor in factors.items():
        out[name] = (out[name] * factor).astype(out[name].dtype)
    return out
```

```python
import math
from contextlib import ExitStack

import concourse.bass as bass
from concourse import mybir

ALU = mybir.AluOpType
ACT = mybir.ActivationFunctionType
AX = mybir.AxisListType
F32 = mybir.dt.float32
F32R = mybir.dt.float32r
I32 = mybir.dt.int32

P = 128
D = 2048
KC = D // P
SEQ = 512
NB = 8
NQ = 8
NS = NB * NQ
NT = SEQ // P
TILES = NT + 1
H = 8
DH = 128
AW = H * DH
PAST = 2048
PAGE = 128
PAGES = PAST // PAGE
G = 64
GC = 16
NST = 64
T = 8
NCH = SEQ // T
NJ = NCH + NB
GP = G // 2
FF = 4 * D
NMOD = 6
ICOLS = 3 * AW + H + AW
ALPHA = 2.0 ** 0.25
SCALE = DH ** -0.5
EPS = 1e-5
NEG = -1.0e30
MAGIC = 1.5 * 2.0 ** 23
TP1 = 6.28125
TP2 = round((2.0 * math.pi - TP1) * 2.0 ** 22) / 2.0 ** 22
TP3 = 2.0 * math.pi - TP1 - TP2
LN1 = 0.693359375
LN2 = math.log(2.0) - LN1

NR = 3
NW = 3
GK = 2
CW = 512
LAG = 3


class Own:

    def __init__(self, eng, sem):
        self.eng, self.sem, self.n = eng, sem, 0

    def __call__(self, ins):
        ins.then_inc(self.sem, 1)
        self.n += 1
        self.eng.wait_ge(self.sem, self.n)


def bank(t, c):
    if t < 3:
        return (2 if c % 2 == 0 or c < 8 else 5) + t
    return t - 3


def program(nc, a, o):
    with ExitStack() as ctx:
        base = 16512
        end = 229368

        def at(name, shape, off, dt=F32):
            n = 4
            for s in shape[1:]:
                n *= s
            assert base + off + n <= end, (name, base + off + n, end)
            return nc.alloc_sbuf_tensor_at(name, shape, dt, offset=base + off)

        REUSED = {"page0": ("ada_full0", 176), "page1": ("ada_full1", 176), "page2": ("ada_full2", 176),
                  "page3": ("adb_full0", 864), "page4": ("c_raw", 256), "page5": ("c_in", 32),
                  "page6": ("bada_in", 16), "page7": ("adb_full1", 848), "page8": ("bf_in", 16),
                  "page9": ("U_in", 128), "page10": ("prm_in", 128), "page11": ("bt_in", 32),
                  "kt_a": ("ada_g", 24), "kt_v": ("ada_m", 24), "kturn_d": ("ada_t", 24),
                  "page_used": ("ada_used", 192), "s_cp": ("p_exp", 32), "s_mx": ("p_mx", 32),
                  "s_done": ("p_s", 32), "n_acc": ("p_acc", 8), "n_ev": ("p_n", 32), "mx": ("lf_w", 1),
                  "d_const": ("hsel", 1), "totl": ("lf_e", 1), "offs": ("f_acc", 1), "D": ("lg", 1),
                  "D_out": ("v_out", 64), "exp": ("p_T", 32), "pt_t": ("p_t", 32), "pt_ev": ("kout", 8),
                  "o_n": ("kturn", 8), "o_T": ("tokT", 3), "o_ev": ("lfT", 1), "z2": ("lfo", 1),
                  "mix_hi": ("X_re", 16), "mix_lo": ("X_im", 16), "mix_lo_v": ("silu", 1), "x1": ("X_t", 16), "r_hi": ("X_T", 16),
                  "r_lo": ("s_acc", 16), "r_sq": ("S_ev", 16), "y_row": ("y_acc", 16), "y_out": ("gelu", 16),
                  "y_acc2": ("glu", 16)}
        sems = {}
        owns = {}

        def B(name):
            return REUSED[name][1] if name in REUSED else 0

        def S(name):
            if name in REUSED:
                name = REUSED[name][0]
            if name not in sems:
                sems[name] = ctx.enter_context(nc.semaphore(name))
            return sems[name]

        pos = [0]

        def const(name, shape, dt=F32):
            n = 4
            for s in shape[1:]:
                n *= s
            t = at(name, shape, pos[0], dt)
            pos[0] += -(-n // 32) * 32
            return t

        W0 = 20224
        ident = const("ident", [P, P])
        diag = const("diag", [P, P])
        badaw = const("badaw", [1, CW])
        scT = const("scT", [P, KC, 32])
        selp = const("selp", [P, P])
        sels = const("sels", [P, NS])
        later = const("later", [P, P])
        modT = const("modT", [P, NMOD * KC, 1 + NB])
        badaT = const("badaT", [P, NMOD * KC])
        ones = const("ones", [1, P])
        stats = const("stats", [P, 4, 6])
        stats5 = const("stats5", [P, TILES, 4, 6])
        mv = const("mv", [P, 2])
        rstd = const("rstd", [P, 2])
        logf = const("logf", [H, SEQ + NS])
        nfc = const("nfc", [H, SEQ + NS])
        keep = const("keep", [H, SEQ + NS])
        bf = const("bf", [H, 1])
        soft = const("soft", [P, 8])
        pages = const("pages", [1, NB * PAGES], I32)
        pageid = const("pageid", [P, 1], I32)
        m8 = const("m8", [P, T])
        assert pos[0] <= W0, pos[0]

        SL = GK * CW * 4
        raw = [at(f"raw{i}", [P, GK, CW], W0 + i * SL) for i in range(NR)]
        whi = [at(f"whi{i}", [P, GK, CW], W0 + (NR + i) * SL, F32R) for i in range(NW)]
        wlo = [at(f"wlo{i}", [P, GK, CW], W0 + (NR + NW + i) * SL, F32R) for i in range(NW)]
        adr = [at(f"adr{i}", [P, GK, CW], W0 + (NR + 2 * NW + i) * SL) for i in range(3)]
        X0 = W0 + (NR + 2 * NW + 3) * SL
        xhi = at("xhi", [P, KC, SEQ], X0, F32R)
        xlo = at("xlo", [P, KC, SEQ], X0 + 32768, F32R)
        xsm = at("xsm", [P, KC, 2 * NS], X0 + 65536, F32R)
        R0 = X0 + 73728
        ps = [ctx.enter_context(nc.psum_tensor(f"ps{i}", [P, 512], F32)) for i in range(8)]

        dram = {}

        def scratch(name, shape):
            dram[name] = nc.dram_tensor(name, shape, F32, kind="Internal").ap()
            return dram[name]

        gate_d = scratch("gate_d", (2, P + NS, D))
        qs_d = scratch("qs_d", (NS, AW))
        us_d = scratch("us_d", (NS, AW))
        u_d = scratch("u_d", (AW, T, NJ))

        crow = at("crow", [1 + NB, D], R0)
        gpart = [at(f"gpart{i}", [P, CW], R0 + 61440 + 2048 * i) for i in range(2)]
        gstage = at("gstage", [P, 2, CW], R0 + 65536)
        badar = at("badar", [NMOD * KC, P], R0 + 16384)
        xrow = [at(f"xrow{i}", [P, D], R0 + 33280 + 8192 * i) for i in range(2)]
        val = [at(f"val{i}", [P, CW], R0 + 49664 + 2048 * i) for i in range(2)]
        qT = at("qT", [P, H, SEQ], R0)
        kT = at("kT", [P, H, SEQ], R0 + 16384)
        vtok = at("vtok", [P, NT, AW], R0 + 32768)
        csum = [at(f"csum{i}", [64, CW], R0 + 49152 + 2048 * i) for i in range(2)]
        ust = at("ust", [P, 4, T, NCH], R0 + 53248)
        qTs = at("qTs", [P, H, NS], R0 + 61440)
        kTs = at("kTs", [P, H, NS], R0 + 63488)
        vs = at("vs", [64, AW], R0 + 65536)
        lf1, lf2, lf3 = (at(f"lf{i}", [H, SEQ + NS], R0 + 53248 + 2304 * i) for i in (0, 1, 2))
        fcum = at("fcum", [H, SEQ + NS], R0 + 60160)
        wfr = at("wfr", [P, KC, H], R0 + 16384)
        wfh = at("wfh", [P, KC, P], R0 + 17408, F32R)
        wfl = at("wfl", [P, KC, P], R0 + 25600, F32R)

        block = ctx.enter_context(nc.Block())

        x_p = a["x_prompt"].rearrange("o s d -> (o s) d")
        x_s = a["x_sample"].rearrange("b q d -> (b q) d")
        wada = a["w_ada"][0]
        win = a["w_in"][0]
        PJ = [("k", AW, 0), ("k", AW + CW, 1), ("q", 0, 0), ("q", CW, 1),
              ("v", 2 * AW, 0), ("v", 2 * AW + CW, 1), ("u", 3 * AW + H, 0), ("u", 3 * AW + H + CW, 1)]
        NGC = KC // GK

        def tile_rows(t):
            return P if t < NT else NS

        def split_act(e, g, gl, first, hid):
            e.wait_ge(S(f"raw_full{gl % NR}"), 16 * (g // NR) + 16)
            if not first:
                e.wait_ge(S("w_used"), g - NW + 1)
            nc.scalar.activation(whi[gl % NW][:, :, :], raw[gl % NR][:, :, :], ACT.Copy).then_inc(S("w_hi"), 1)

        def split_dve(e, g, gl):
            e.wait_ge(S("w_hi"), g + 1)
            nc.vector.tensor_tensor(wlo[gl % NW][:, :, :], raw[gl % NR][:, :, :],
                                    whi[gl % NW][:, :, :].bitcast(F32), ALU.subtract).then_inc(S("w_lo"), 1)

        def load_w(e, g, gl, src, first):
            if not first:
                e.wait_ge(S("w_lo"), g - NR + 1)
            e.dma_start(raw[gl % NR][:, :, :], src.rearrange("(k p) n -> p k n", p=P)).then_inc(
                S(f"raw_full{gl % NR}"), 16)

        def pe_chunk(e, c, g0, gl0, kinds, nk, hi, lo, sm, free, after=None, need=None):
            for gi in range(nk // GK):
                e.wait_ge(S("w_lo"), g0 + gi + 1)
                hw, lw = whi[(gl0 + gi) % NW], wlo[(gl0 + gi) % NW]
                for k2 in range(GK):
                    k = gi * GK + k2
                    for t in range(TILES):
                        if need is not None and t in (0, NT):
                            need(k, t)
                        if k == 0 and free is not None:
                            free(e, t)
                        acc = ps[bank(t, c)]
                        st, en = k == 0, k == nk - 1
                        if t < NT and kinds == "w":
                            n = slice(t * P, t * P + P)
                            nc.tensor.matmul(acc[:, :], hw[:, k2, n], hi[:, k, :], start=st, stop=False)
                            nc.tensor.matmul(acc[:, :], hw[:, k2, n], lo[:, k, :], start=False, stop=False)
                            mm = nc.tensor.matmul(acc[:, :], lw[:, k2, n], hi[:, k, :], start=False, stop=en)
                        elif t < NT:
                            n = slice(t * P, t * P + P)
                            nc.tensor.matmul(acc[:, :], hi[:, k, n], hw[:, k2, :], start=st, stop=False)
                            nc.tensor.matmul(acc[:, :], lo[:, k, n], hw[:, k2, :], start=False, stop=False)
                            mm = nc.tensor.matmul(acc[:, :], hi[:, k, n], lw[:, k2, :], start=False, stop=en)
                        else:
                            nc.tensor.matmul(acc[:, :], sm[:, k, :], hw[:, k2, :], start=st, stop=False)
                            mm = nc.tensor.matmul(acc[:, :], sm[:, k, :], lw[:, k2, :], start=False, stop=en)
                            if k2 == GK - 1:
                                mm.then_inc(S("w_used"), 1)
                        if en and t < NT:
                            mm.then_inc(S(f"acc{t}"), 1)
                if after is not None:
                    after(g0 + gi)

        def norm_dve(e, own, name, src, t, wait, rnd=0, dst=None, st=None):
            r = tile_rows(t)
            wait()
            if (rnd, t) == (0, 1):
                e.wait_ge(S("a_xn"), 1)
            n = TILES * rnd + t + 1 if rnd == 0 or rnd == 3 else TILES + 2 * t + rnd
            if st is None:
                for i in range(4):
                    ins = nc.vector.bn_stats(stats[0:r, i, :], src[0:r, i * 512:i * 512 + 512])
                own(ins)
                st = stats[0:r, :, :]
            own(nc.vector.bn_aggr(mv[0:r, :], st.rearrange("p a b -> p (a b)")))
            nc.vector.tensor_scalar(rstd[0:r, 0:1], mv[0:r, 1:2], EPS, None, ALU.add).then_inc(S(name + "_var"), 1)
            e.wait_ge(S(name + "_std"), n)
            own(nc.vector.reciprocal(rstd[0:r, 1:2], rstd[0:r, 0:1]))
            dst = src[0:r, :] if dst is None else dst
            return nc.vector.tensor_scalar(dst, src[0:r, :], mv[0:r, 0:1], rstd[0:r, 1:2],
                                           ALU.subtract, ALU.mult)

        def norm_act(e, name, t, rnd=0):
            r = tile_rows(t)
            n = TILES * rnd + t + 1 if rnd == 0 or rnd == 3 else TILES + 2 * t + rnd
            e.wait_ge(S(name + "_var"), n)
            nc.scalar.activation(rstd[0:r, 0:1], rstd[0:r, 0:1], ACT.Sqrt).then_inc(S(name + "_std"), 1)

        GROUPS = [(t, q) for t in range(NT) for q in range(4)] + [(NT, 0), (NT, 1)]

        def turn_pe(e, name, src, t, rnd=0):
            e.wait_ge(S(name + "_xn"), TILES * rnd + t + 1)
            for i, (tt, q) in enumerate(GROUPS):
                if tt != t:
                    continue
                if i >= 2 or rnd:
                    e.wait_ge(S(name + "_val"), NGR * rnd + i - 1)
                if t < NT:
                    for b in range(4):
                        mm = nc.tensor.transpose(ps[i % 2][:, b * P:b * P + P],
                                                 src[:, (4 * q + b) * P:(4 * q + b + 1) * P], ident[:, :])
                else:
                    for b in range(8):
                        mm = nc.tensor.transpose(ps[i % 2][:, b * NS:b * NS + NS],
                                                 src[0:NS, (8 * q + b) * P:(8 * q + b + 1) * P], ident[0:NS, 0:NS])
                mm.then_inc(S(name + "_turn"), 1)

        def turn_dve(e, own, name, t, shift, rnd=0):
            for i, (tt, q) in enumerate(GROUPS):
                if tt != t:
                    continue
                e.wait_ge(S(name + "_turn"), NGR * rnd + i + 1)
                if i >= 2 or rnd:
                    e.wait_ge(S(name + "_lo"), NGR * rnd + i - 1)
                v = (val2 if rnd else val)[i % 2]
                if t < NT:
                    for b in range(4):
                        k = 4 * q + b
                        ins = nc.vector.tensor_scalar(
                            v[:, b * P:b * P + P], ps[i % 2][:, b * P:b * P + P],
                            modT[:, (shift + 1) * KC + k, 0:1], modT[:, shift * KC + k, 0:1], ALU.mult, ALU.add)
                    ins.then_inc(S(name + "_val"), 1)
                else:
                    ks = slice(8 * q, 8 * q + 8)
                    shape = [P, 8, NB, NQ]
                    vv = v[:, :].rearrange("p (k b q) -> p k b q", k=8, b=NB)
                    sc = modT[:, (shift + 1) * KC + 8 * q:(shift + 1) * KC + 8 * q + 8, 1:1 + NB]
                    sh = modT[:, shift * KC + 8 * q:shift * KC + 8 * q + 8, 1:1 + NB]
                    own(nc.vector.tensor_tensor(vv, ps[i % 2][:, :].rearrange("p (k b q) -> p k b q", k=8, b=NB),
                                                sc.unsqueeze(3).to_broadcast(shape), ALU.mult))
                    nc.vector.tensor_tensor(vv, vv, sh.unsqueeze(3).to_broadcast(shape),
                                            ALU.add).then_inc(S(name + "_val"), 1)

        def turn_dst(i, half):
            t, q = GROUPS[i]
            if t < NT:
                return (xhi, xlo)[half][:, 4 * q:4 * q + 4, t * P:t * P + P]
            return xsm[:, 8 * q:8 * q + 8, half * NS:half * NS + NS]

        def turn_src(i, rnd):
            t, _ = GROUPS[i]
            return (val2 if rnd else val)[i % 2][:, :].rearrange("p (k n) -> p k n", k=4 if t < NT else 8)

        def turn_act(e, name, i, rnd=0):
            e.wait_ge(S(name + "_val"), NGR * rnd + i + 1)
            nc.scalar.activation(turn_dst(i, 0), turn_src(i, rnd), ACT.Copy).then_inc(S(name + "_hi"), 1)

        def turn_pool(e, name, i, rnd=0):
            e.wait_ge(S(name + "_hi"), NGR * rnd + i + 1)
            nc.gpsimd.tensor_tensor(turn_dst(i, 1), turn_src(i, rnd), turn_dst(i, 0).bitcast(F32),
                                    ALU.subtract).then_inc(S(name + "_lo"), 1)

        NGR = len(GROUPS)
        ADA = NMOD * D // CW
        ADA1 = 2 * D // CW
        GATES = [2, 5]

        ADA_FULL = [f"ada_full{i}" for i in range(3)] + [f"adb_full{i}" for i in range(3)]
        ADB0 = [16 * len(range(3 + i, ADA1 * KC // GK, 6)) for i in range(3)]

        def gate_index(m):
            return 4 * GATES.index(m // 4) + m % 4 if m // 4 in GATES else None

        def ada_events(x):
            n, ph = ADA1 + x // 4, x % 4
            if ph == 2 and n > ADA1:
                return "turn", n - 1
            if ph == 3 and n > ADA1 and gate_index(n - 1) is not None:
                return "prompt", n - 1
            if ph == 0 and n > ADA1 + 1 and gate_index(n - 2) is not None:
                return "sample", n - 2
            return None

        ADA_END = [("sample", ADA - 2), ("turn", ADA - 1), ("prompt", ADA - 1), ("sample", ADA - 1)]
        NGP = 64

        def ada_ready(e):
            e.wait_ge(S("ada_g"), ADA)
            e.wait_ge(S("ada_m"), ADA)
            e.wait_ge(S("gate_row"), 16)
            e.wait_ge(S("gate_out"), 256)

        def gate_dma(e, ev):
            kind, m = ev
            i = gate_index(m)
            if kind == "turn":
                return
            q = m % 4
            cols = slice(q * CW, q * CW + CW)
            sm = kind == "sample"
            e.wait_ge(S("gate_row"), 2 * i + 1 + sm)
            rows = slice(P, P + NS) if sm else slice(0, P)
            e.dma_start(gate_d[i // 4, rows, cols], gstage[0:NS if sm else P, int(sm), :]).then_inc(S("gate_out"), 16)
            if sm and i < 7:
                bias_in(e, i + 1)

        def bias_in(e, i):
            if i:
                e.wait_ge(S("gate_acc"), 2 * i)
            col = GATES[i // 4] * D + i % 4 * CW
            e.dma_start(badaw[:, :], a["b_ada"][0:1, col:col + CW]).then_inc(S("badaw_in"), 16)

        def ada_evac(e, own, ev):
            kind, m = ev
            i = gate_index(m)
            if kind == "turn":
                e.wait_ge(S("ada_t"), m + 1)
                m4 = modT[:, 4 * m:4 * m + 4, :]
                own(nc.vector.tensor_reduce(
                    m4, ps[7][:, :].rearrange("p (b j i) -> p b i j", b=4, j=4)[:, :, 0:9, :], AX.X, ALU.add))
                nc.vector.tensor_tensor(m4, m4, badaT[:, 4 * m:4 * m + 4].unsqueeze(2).to_broadcast([P, 4, 9]),
                                        ALU.add).then_inc(S("ada_m"), 1)
                return
            sm = kind == "sample"
            r = NS if sm else P
            e.wait_ge(S("gate_acc"), 2 * i + 1 + sm)
            if i:
                e.wait_ge(S("gate_out"), 32 * i)
            nc.vector.tensor_scalar(gstage[0:r, int(sm), :], ps[7][0:r, :], 1.0, None, ALU.add).then_inc(
                S("gate_row"), 1)

        def ada_event_pe(e, ev):
            kind, m = ev
            i = gate_index(m)
            if kind == "turn":
                e.wait_ge(S("ada_g"), m + 1)
                e.wait_ge(S("ada_m"), m)
                done = sum(2 for k in range(ADA1, m) if gate_index(k) is not None)
                if done:
                    e.wait_ge(S("gate_row"), done)
                for b in range(4):
                    mm = nc.tensor.transpose(ps[7][:, b * P:b * P + P], gpart[m % 2][:, b * P:b * P + P], ident[:, :])
                mm.then_inc(S("ada_t"), 1)
                return
            sm = kind == "sample"
            if sm:
                e.wait_ge(S("gate_row"), 2 * i + 1)
            else:
                e.wait_ge(S("ada_m"), m + 1)
                e.wait_ge(S("badaw_in"), 16 * i + 16)
            r = NS if sm else P
            w = sels if sm else selp
            nc.tensor.matmul(ps[7][0:r, :], w[:, :], gpart[m % 2][:, :], start=True, stop=False)
            nc.tensor.matmul(ps[7][0:r, :], ones[:, 0:r], badaw[:, :], start=False, stop=True).then_inc(
                S("gate_acc"), 1)

        def ada_slot(e, x):
            n, ph = ADA1 + x // 4, x % 4
            if ph == 0 and n >= ADA1 + 2:
                e.wait_ge(S("ada_g"), n - 1)
            for q in (2 * ph, 2 * ph + 1):
                g = (n - ADA1) * NGC + q
                e.wait_ge(S(f"adb_full{g % 3}"), ADB0[g % 3] + 16 * (g // 3) + 16)
                for k2 in range(GK):
                    k = q * GK + k2
                    j = k % 4
                    mm = nc.tensor.matmul(ps[5 + n % 2][32 * j:32 * j + 32, :], scT[:, k, :], adr[g % 3][:, k2, :],
                                          start=k < 4, stop=k >= KC - 4)
                mm.then_inc(S("ada_used"), 1)
            ev = ada_events(x)
            if ev:
                ada_event_pe(e, ev)

        tok = at("tok", [64, 3, AW], X0)
        usb = at("usb", [P, 8, NQ, NB], X0 + 12288)
        lfo = at("lfo", [P, TILES, H], X0 + 14336)
        kout = [at(f"kout{i}", [P, AW], X0 + 16384 + 4096 * i) for i in range(2)]
        hsel = at("hsel", [H, H, P], X0 + 24576)
        pb = [at(f"pb{i}", [P, 4, 512], X0 + 28672 + 8192 * i) for i in range(2)]
        pT = [at(f"pT{i}", [P, 4, 512], X0 + 45056 + 8192 * i) for i in range(2)]
        pmx = at("pmx", [P, 4 * H], X0 + 61440)
        psum_ = at("psum_", [P, 4 * H], X0 + 61568)
        prc = at("prc", [P, 4 * H], X0 + 61696)
        NGT = len(PJ) * NGC

        def p_sp(e):
            ada_ready(e)
            e.wait_ge(S("csum_out0"), 64)
            e.wait_ge(S("csum_out1"), 64)
            e.wait_ge(S("w_used"), NGT)
            for i, src in enumerate([qs_d, o["k_sample"][0].rearrange("b q h d -> (b q) (h d)"), us_d]):
                e.dma_start(tok[:, i, :], src).then_inc(S("tok_in"), 16)
            e.dma_start(vs[:, :], o["v_sample"][0].rearrange("b q h d -> (b q) (h d)")).then_inc(S("tok_in"), 16)
            e.wait_ge(S("ust_out"), 128)
            for i, n in enumerate(["a_re", "a_im"]):
                e.dma_start(prmr[:, i, :], a[n][0].rearrange("(gp r) n -> gp (r n)", r=2)).then_inc(S("prm_in"), 16)
            e.dma_start(ldi[:, :], a["log_dt"]).then_inc(S("prm_in"), 16)
            e.dma_start(d32i[:, :], a["d_skip"][0].rearrange("(gp r) c -> gp (r c)", r=2)).then_inc(S("prm_in"), 16)
            e.dma_start(bgi[:, :, :], a["b_glu"][0].rearrange("g (h e) -> g h e", h=2)).then_inc(S("bg_in"), 16)

        def p_pool(e):
            own = owns["pool"]
            e.wait_ge(S("w_used"), NGT)
            nc.gpsimd.tensor_copy(hsel[:, :, :], ident[0:H, 0:H].unsqueeze(2).to_broadcast([H, H, P])).then_inc(
                S("hsel"), 1)
            ada_ready(e)
            own(nc.gpsimd.tensor_tensor(eye16[:, :], ident[0:32, 0:16], ident[0:32, 16:32], ALU.add))
            e.wait_ge(S("bg_in"), 16)
            nc.gpsimd.tensor_copy(bgr[:, :, :, :], bgi[:, :, :].unsqueeze(2).to_broadcast([G, 2, T, GC])).then_inc(
                S("eye16"), 1)
            e.wait_ge(S("usb"), 1)
            for k in range(8):
                e.dma_start(u_d[k * P:k * P + P, :, NCH:NJ], usb[:, k, :, :]).then_inc(S("usb_out"), 16)
            e.wait_ge(S("lfo"), 1)
            e.dma_start(o["logf_prompt"][0, 0].rearrange("(t p) h -> p t h", p=P), lfo[:, 0:NT, :]).then_inc(
                S("lf_out"), 16)
            e.dma_start(o["logf_sample"][0].rearrange("b q h -> (b q) h"), lfo[0:NS, NT, :]).then_inc(S("lf_out"), 16)
            for t in range(NT):
                e.wait_ge(S("kout"), 2 * t + 2)
                e.dma_start(o["k_prompt"][0, 0, t * P:t * P + P].rearrange("s h d -> s (h d)"),
                            kout[t % 2][:, :]).then_inc(S(f"k_out{t % 2}"), 16)
            e.wait_ge(S("lf_out"), 32)
            e.wait_ge(S("usb_out"), 128)
            e.wait_ge(S("k_out0"), 32)
            e.wait_ge(S("k_out1"), 32)

        def p_pe(e):
            e.wait_ge(S("tok_in"), 64)
            ada_ready(e)
            for t in range(NT):
                e.wait_ge(S(f"out{t}"), len(PJ))
            e.wait_ge(S("csum"), len(PJ))
            for i in range(3):
                for b in range(8):
                    mm = nc.tensor.transpose(ps[2 + i][:, b * 64:b * 64 + 64], tok[:, i, b * P:b * P + P],
                                             ident[0:64, 0:64])
                mm.then_inc(S("tokT"), 1)
            e.wait_ge(S("prm_in"), 64)
            e.wait_ge(S("eye16"), 1)
            for i in range(2):
                nc.tensor.transpose(ps[0][:, i * 32:i * 32 + 32], prmr[:, i, :], ident[0:GP, 0:GP])
            nc.tensor.matmul(ps[0][:, 64:128], ones[:, :], ldi[:, :], start=True, stop=True)
            nc.tensor.transpose(ps[0][0:32, 256:288], d32i[:, :], ident[0:GP, 0:GP])
            for i in range(2):
                mm = nc.tensor.transpose(ps[0][:, 128 + 64 * i:192 + 64 * i], bgr[:, i, :, :].rearrange("g t e -> g (t e)"),
                                    ident[0:G, 0:G])
            mm.then_inc(S("prm_T"), 1)
            e.wait_ge(S("fcum"), 1)
            for t in range(NT):
                nc.tensor.transpose(ps[5][:, t * H:t * H + H], logf[:, t * P:t * P + P], ident[0:H, 0:H])
            nc.tensor.transpose(ps[5][0:NS, NT * H:NT * H + H], logf[:, SEQ:], ident[0:H, 0:H]).then_inc(S("lfT"), 1)
            for n in range(2 * NT):
                t, hh = n // 2, n % 2
                if n >= 2:
                    e.wait_ge(S("kout"), n - 1)
                for b in range(4):
                    mm = nc.tensor.transpose(ps[6 + n % 2][:, b * P:b * P + P],
                                             kT[:, 4 * hh + b, t * P:t * P + P], ident[:, :])
                mm.then_inc(S("kturn"), 1)
            e.wait_ge(S("hsel"), 1)
            e.wait_ge(S("tok_ev"), 2)
            e.wait_ge(S("usb"), 1)
            e.wait_ge(S("kout"), 2 * NT)
            e.wait_ge(S("lfo"), 1)
            e.wait_ge(S("prm_ev"), 1)

            def scores(h):
                for i in range(NT):
                    w = (i + 1) * P
                    if h >= 1:
                        e.wait_ge(S("p_exp"), 4 * (h - 1) + i + 1)
                    nc.tensor.matmul(ps[i][:, 0:w], qT[:, h, i * P:i * P + P], kT[:, h, 0:w], start=True, stop=False)
                    nc.tensor.matmul(ps[i][:, 0:w], hsel[:, h, :], nfc[:, 0:w], start=False, stop=True).then_inc(
                        S("p_s"), 1)

            def turn(h):
                for i in range(NT):
                    n = 4 * h + i
                    e.wait_ge(S("p_n"), n + 1)
                    if n >= 2:
                        e.wait_ge(S("p_T"), n - 1)
                    for k in range(i + 1):
                        mm = nc.tensor.transpose(ps[4 + i % 2][:, k * P:k * P + P], pb[h % 2][:, i, k * P:k * P + P],
                                                 ident[:, :])
                    mm.then_inc(S("p_t"), 1)

            def values(h):
                e.wait_ge(S("p_T"), 4 * h + 4)
                if h >= 2:
                    e.wait_ge(S("p_o"), h - 1)
                for k in range(NT):
                    mm = nc.tensor.matmul(ps[6 + h % 2][:, k * P:SEQ], vtok[:, k, h * DH:h * DH + DH],
                                          pT[h % 2][:, k, k * P:SEQ], start=k == 0, stop=k == NT - 1,
                                          skip_group_check=True)
                mm.then_inc(S("p_acc"), 1)

            scores(0)
            for h in range(H):
                if h + 1 < H:
                    scores(h + 1)
                turn(h)
                values(h)

        def p_dve(e):
            own = owns["dve"]
            ada_ready(e)
            for i, dst in enumerate([qTs, kTs]):
                e.wait_ge(S("tokT"), i + 1)
                nc.vector.tensor_scalar(dst[:, :, :], ps[2 + i][:, :].rearrange("p (b n) -> p b n", b=8),
                                        SCALE if i == 0 else 1.0, None, ALU.mult).then_inc(S("tok_ev"), 1)
            e.wait_ge(S("tokT"), 3)
            nc.vector.tensor_copy(usb[:, :, :, :], ps[4][:, :].rearrange("p (k b t) -> p k t b", k=8, b=NB)).then_inc(
                S("usb"), 1)
            e.wait_ge(S("lfT"), 1)
            own(nc.vector.tensor_copy(lfo[:, 0:NT, :], ps[5][:, 0:NT * H].rearrange("p (t h) -> p t h", h=H)))
            nc.vector.tensor_copy(lfo[0:NS, NT, :], ps[5][0:NS, NT * H:NT * H + H]).then_inc(S("lfo"), 1)
            e.wait_ge(S("csum_out0"), 64)
            e.wait_ge(S("csum_out1"), 64)
            e.wait_ge(S("ust_out"), 128)
            prm_rows(e)

            def maxima(h):
                for i in range(NT):
                    n = 4 * h + i
                    e.wait_ge(S("p_s"), n + 1)
                    d = ps[i][:, i * P:i * P + P]
                    own(nc.vector.tensor_tensor(d, d, diag[:, :], ALU.add))
                    nc.vector.tensor_reduce(pmx[:, n:n + 1], ps[i][:, 0:(i + 1) * P], AX.X, ALU.max,
                                            negate=True).then_inc(S("p_mx"), 1)

            maxima(0)
            for h in range(H):
                if h + 1 < H:
                    maxima(h + 1)
                for i in range(NT):
                    n = 4 * h + i
                    e.wait_ge(S("p_exp"), n + 1)
                    own(nc.vector.reciprocal(prc[:, n:n + 1], psum_[:, n:n + 1]))
                    w = pb[h % 2][:, i, 0:(i + 1) * P]
                    nc.vector.tensor_scalar(w, w, prc[:, n:n + 1], None, ALU.mult).then_inc(S("p_n"), 1)
                if h == 1:
                    prm_exp(e, own)
                if h == 2:
                    prm_angle(e, own)
                if h == 3:
                    prm_gain(e, own)
                if h == 4:
                    prm_powers(e, own)

        def p_act(e):
            for n in range(2 * NT):
                t, hh = n // 2, n % 2
                e.wait_ge(S("kturn"), n + 1)
                if t >= 2:
                    e.wait_ge(S(f"k_out{t % 2}"), 16)
                nc.scalar.activation(kout[t % 2][:, hh * 512:hh * 512 + 512], ps[6 + n % 2][:, :], ACT.Copy).then_inc(
                    S("kout"), 1)

            def exps(h):
                if h >= 2:
                    e.wait_ge(S("p_t"), 4 * (h - 1))
                for i in range(NT):
                    n = 4 * h + i
                    e.wait_ge(S("p_mx"), n + 1)
                    w = (i + 1) * P
                    nc.scalar.activation(pb[h % 2][:, i, 0:w], ps[i][:, 0:w], ACT.Exp, bias=pmx[:, n:n + 1],
                                         accum_out=psum_[:, n:n + 1]).then_inc(S("p_exp"), 1)

            exps(0)
            for h in range(H):
                if h + 1 < H:
                    exps(h + 1)
                if h >= 2:
                    e.wait_ge(S("p_acc"), h - 1)
                for i in range(NT):
                    n = 4 * h + i
                    e.wait_ge(S("p_t"), n + 1)
                    nc.scalar.activation(pT[h % 2][:, 0:i + 1, i * P:i * P + P],
                                         ps[4 + i % 2][:, 0:(i + 1) * P].rearrange("p (k n) -> p k n", n=P),
                                         ACT.Copy).then_inc(S("p_T"), 1)
                e.wait_ge(S("p_acc"), h + 1)
                nc.scalar.activation(qT[:, h, :], ps[6 + h % 2][:, :], ACT.Copy).then_inc(S("p_o"), 1)

        kpad_d = scratch("kpad_d", (G, GC, 15 * GC))
        zs_d = scratch("zs_d", (AW, T, NJ))
        GH = GP // 2
        Y = [at(f"Y{i}", [P, GP, T + 1, GC], W0 + 18432 * i) for i in range(2)]
        Sj = at("Sj", [P, NJ, 2, GP], W0 + 36864)
        ytmp = [at(f"ytmp{i}", [P, GH, T + 1, GC], W0 + 36864 + 9216 * i) for i in range(2)]
        expi = at("expi", [P, GP], W0 + 36864 + 8192, I32)
        Z = at("Z", [P, G, NJ], W0 + 36864)
        Hz = at("Hz", [P, GP, 2, 2, NJ], W0 + 55296)
        craw = at("craw", [P, 2, 4, P], W0 + 55296)
        Kst = at("Kst", [32, GP, T * GC], W0 + 59392)
        Kbd = at("Kbd", [P, 2, GP, 32], W0 + 75776)
        zt = at("zt", [P, 8, 112], W0 + 83968)
        U = at("U", [P, G, NJ], W0 + 92160)
        Xn = [at(f"Xn{i}", [P, 2, 2, T, GC], W0 + 110592 + 2048 * i) for i in range(2)]
        XT = [at(f"XT{i}", [P, 4, P], W0 + 114688 + 2048 * i) for i in range(2)]
        xtmp = at("xtmp", [P, 2, T, GC], W0 + 118784)
        xtmp2 = at("xtmp2", [P, 2, T, GC], W0 + 119808)
        bd = [at(f"bd{i}", [P, 2, T, GC], W0 + 120832 + 1024 * i) for i in range(2)]
        wrep = at("wrep", [P, G, 2 * GC], W0 + 110592)
        Hst = at("Hst", [P, NCH + 1, 2, GP], R0 + 16384)
        bb = at("bb", [P, 2, GP, GC], R0 + 33280)
        bt = at("bt", [P, 2, GP, GC], R0 + 37376)
        cc = at("cc", [P, 2, GP, GC], R0 + 41472)
        Mb = [at(f"Mb{i}", [P, 8, P], R0 + 33280 + 4096 * i) for i in range(3)]
        P9 = at("P9", [P, T + 1, 2, GP], R0 + 49664)
        PR = at("PR", [P, 2, GP, T], R0 + 45568)
        hs = at("hs", [P, 2, NB, GP], R0 + 47616)
        prm = at("prm", [P, 16, GP], R0 + 51968)
        rt = at("rt", [P, 2, 2, GP], R0 + 54016)
        prmr = at("prmr", [GP, 2, P], R0 + 54528)
        h0 = at("h0", [P, 2, NB, GP], R0 + 56064)
        bgr = at("bgr", [G, 2, T, GC], R0 + 58112)
        bgi = at("bgi", [G, 2, GC], R0 + 59136)
        bgT = at("bgT", [P, 2, G], R0 + 59264)
        d32 = at("d32", [32, GP], R0 + 59776)
        d32i = at("d32i", [GP, 32], R0 + 59904)
        ldi = at("ldi", [1, G], R0 + 60032)
        eye16 = at("eye16", [32, GC], R0 + 60288)
        dT = at("dT", [32, GC], R0 + 60352)
        L16 = at("L16", [P, 2, GP], R0 + 60416)
        h0r = at("h0r", [P, 2, 2, P], R0 + 16384)
        hout = at("hout", [P, 2, 3, P], R0 + 37376)
        gl1 = [at(f"gl1_{i}", [P, 4, NJ], W0 + 55296 + 1152 * i) for i in range(2)]
        gl2 = [at(f"gl2_{i}", [P, 4, NJ], W0 + 57600 + 1152 * i) for i in range(2)]
        Zo = at("Zo", [P, G, NJ], W0 + 92160)
        zr = at("zr", [P, 8, T, NJ], R0 + 16384)
        NX = GP // 2

        def p_done(e):
            e.wait_ge(S("p_o"), H)
            e.wait_ge(S("tok_ev"), 2)
            e.wait_ge(S("k_out0"), 32)
            e.wait_ge(S("k_out1"), 32)
            e.wait_ge(S("lf_out"), 32)
            e.wait_ge(S("usb_out"), 128)
            e.wait_ge(S("ust_out"), 128)
            e.wait_ge(S("v_out"), 64)

        def s_sp(e):
            p_done(e)
            for i, n in enumerate(["state_ssm_re", "state_ssm_im"]):
                for k in range(2):
                    e.dma_start(h0r[:, i, k, :], a[n][0, 4 * k:4 * k + 4].rearrange(
                        "b (gp r) n -> (b gp) (r n)", r=2)).then_inc(S("prm_in"), 16)
            for i, n in enumerate(["b_re", "b_im"]):
                e.dma_start(bt[:, i, :, :], a[n][0].rearrange("(gp r) n c -> (r n) gp c", r=2)).then_inc(
                    S("bt_in"), 16)
            for i, n in enumerate(["c_re", "c_im"]):
                for k in range(4):
                    for r in range(2):
                        e.dma_start(craw[:, i, k, r * 64:r * 64 + 64],
                                    a[n][0].rearrange("(gp r) c n -> r gp c n", r=2)[r, 8 * k:8 * k + 8]).then_inc(
                            S("c_raw"), 16)
            for s in range(T):
                e.dma_start(U[s * GC:s * GC + GC, :, :], u_d.rearrange("(g c) s j -> s c g j", c=GC)[s]).then_inc(
                    S("U_in"), 16)
            e.wait_ge(S("zt"), 1)
            e.dma_start(kpad_d.rearrange("g c w -> (g c) w").rearrange("(p x) w -> p x w", p=P)[:, :, 0:112],
                        zt[:, :, :]).then_inc(S("k_out"), 16)
            e.wait_ge(S("K_ev"), 8)
            e.dma_start(kpad_d.rearrange("(gp r) c w -> (r c) gp w", r=2)[:, :, 112:240], Kst[:, :, :]).then_inc(
                S("k_out"), 16)
            e.wait_ge(S("k_out"), 32)
            e.wait_ge(S("X_re"), NX)
            e.wait_ge(S("X_im"), NX)
            for b in range(8):
                if b >= 3:
                    e.wait_ge(S("y_acc"), 2 * (b - 2))
                for s in range(T):
                    w = (T - 1 - s) * GC
                    e.dma_start(Mb[b % 3][s * GC:s * GC + GC, :, :],
                                kpad_d[8 * b:8 * b + 8, :, w:w + P].rearrange("g c w -> c g w")).then_inc(
                        S(f"M_in{b % 3}"), 16)
                if b == 2:
                    e.wait_ge(S("s_acc"), NX)
                    for t in range(T):
                        e.dma_start(wrep[t * GC:t * GC + GC, :, :], a["w_glu"][0].rearrange("g c e -> c g e")).then_inc(
                            S("wrep"), 16)
            e.wait_ge(S("h_out"), 3)
            for i, n in enumerate(["ssm_re", "ssm_im"]):
                for k in range(2):
                    e.dma_start(o[n + "_sample"][0, 4 * k:4 * k + 4].rearrange("b (gp r) n -> (b gp) (r n)", r=2),
                                hout[:, i, k, :]).then_inc(S("st_out"), 16)
                e.dma_start(o[n + "_prompt"][0, 0].rearrange("(gp r) n -> gp (r n)", r=2),
                            hout[0:GP, i, 2, :]).then_inc(S("st_out"), 16)
            e.wait_ge(S("st_out"), 96)
            e.wait_ge(S("y_acc"), 16)
            cache_pages(e, range(9))
            e.wait_ge(S("glu"), 16)
            for t in range(T):
                e.dma_start(zs_d.rearrange("(g e) t j -> t e g j", e=GC)[t], Zo[t * GC:t * GC + GC, :, :]).then_inc(
                    S("z_out"), 16)
            e.wait_ge(S("z_out"), 128)
            e.dma_start(zr[:, :, :, :].rearrange("p k t j -> p k (t j)"),
                        zs_d.rearrange("(k f) t j -> f k (t j)", f=P)).then_inc(S("zr_in"), 16)

        def s_pe(e):
            p_done(e)
            e.wait_ge(S("prm_in"), 128)
            for i in range(2):
                for k in range(2):
                    mm = nc.tensor.transpose(ps[1][:, (2 * i + k) * P:(2 * i + k + 1) * P], h0r[:, i, k, :], ident[:, :])
            mm.then_inc(S("prm_T"), 1)
            e.wait_ge(S("c_raw"), 256)
            for i in range(2):
                for k in range(4):
                    mm = nc.tensor.transpose(ps[2 + i][:, k * P:k * P + P], craw[:, i, k, :], ident[:, :])
            mm.then_inc(S("c_T"), 1)
            e.wait_ge(S("Y_re"), 1)
            e.wait_ge(S("Y_im"), 2)
            e.wait_ge(S("Kbd"), 1)
            for b in range(8):
                if b >= 2:
                    e.wait_ge(S("K_ev"), b - 1)
                for q in range(4):
                    gp = 4 * b + q
                    for i in range(2):
                        mm = nc.tensor.matmul(ps[4 + b % 2][0:32, q * P:q * P + P], Kbd[:, i, gp, :],
                                              Y[i][:, gp, 0:T, :], start=i == 0, stop=i == 1)
                mm.then_inc(S("K_acc"), 1)
            e.wait_ge(S("U_in"), 128)
            e.wait_ge(S("s_prm"), 1)

            def turn(b):
                e.wait_ge(S("X_re"), b + 1)
                e.wait_ge(S("X_im"), b + 1)
                if b >= 2:
                    e.wait_ge(S("X_T"), b - 1)
                for q in range(2):
                    for i in range(2):
                        mm = nc.tensor.transpose(ps[6 + b % 2][:, (2 * q + i) * P:(2 * q + i + 1) * P],
                                                 Xn[b % 2][:, i, q, :, :].rearrange("p s c -> p (s c)"), ident[:, :])
                mm.then_inc(S("X_t"), 1)

            def inputs(b):
                e.wait_ge(S("X_T"), b + 1)
                if b >= 2:
                    e.wait_ge(S("S_ev"), b - 1)
                for q in range(2):
                    for i in range(2):
                        for r in range(2):
                            g = 2 * (2 * b + q) + r
                            mm = nc.tensor.matmul(ps[b % 2][r * 64:r * 64 + 64, (2 * q + i) * NJ:(2 * q + i + 1) * NJ],
                                                  XT[b % 2][:, 2 * q + i, r * 64:r * 64 + 64], U[:, g, :],
                                                  start=True, stop=True)
                mm.then_inc(S("s_acc"), 1)

            turn(0)
            for b in range(NX):
                if b + 1 < NX:
                    turn(b + 1)
                inputs(b)
            e.wait_ge(S("Hz"), 3)
            for b in range(16):
                e.wait_ge(S(f"M_in{b // 2 % 3}"), 128 * (b // 6) + 128)
                if b >= 4:
                    e.wait_ge(S("gelu"), b - 3)
                for q in range(4):
                    g = 4 * b + q
                    gp, r = g // 2, g % 2
                    acc = ps[2 + b % 4][:, q * NJ:q * NJ + NJ]
                    nc.tensor.matmul(acc, Mb[b // 2 % 3][:, g % 8, :], U[:, g, :], start=True, stop=False)
                    for i in range(2):
                        mm = nc.tensor.matmul(acc, Y[i][:, gp, 1:T + 1, :], Hz[:, gp, i, r, :], start=False,
                                              stop=i == 1)
                mm.then_inc(S("y_acc"), 1)
            e.wait_ge(S("hs"), 1)
            e.wait_ge(S("S_ev"), NX)
            for i in range(2):
                for k in range(2):
                    nc.tensor.transpose(ps[0][:, (2 * i + k) * P:(2 * i + k + 1) * P],
                                        hs[:, i, 4 * k:4 * k + 4, :].rearrange("p b g -> p (b g)"), ident[:, :])
                mm = nc.tensor.transpose(ps[1][0:GP, i * P:i * P + P], Hst[:, NCH, i, :], ident[:, :])
            mm.then_inc(S("h_T"), 1)
            e.wait_ge(S("gelu"), 16)
            for b in range(16):
                if b >= 3:
                    e.wait_ge(S("glu"), b - 2)
                for q in range(4):
                    g = 4 * b + q
                    e.wait_ge(S("bd"), g + 1)
                    for i in range(2):
                        mm = nc.tensor.matmul(ps[2 + 2 * (b % 3) + i][:, q * NJ:q * NJ + NJ],
                                              bd[g % 2][:, i, :, :].rearrange("p t e -> p (t e)"), Z[:, g, :],
                                              start=True, stop=True)
                    mm.then_inc(S("bd_used"), 1)

        def s_pool(e):
            own = owns["pool"]
            p_done(e)
            e.dma_start(pageid[:, :], a["page_table"].rearrange("b (k o) -> (b k) o", o=1)).then_inc(S("pageid"), 16)
            e.dma_start(pages[:, :], a["page_table"].rearrange("(o b) k -> o (b k)", o=1)).then_inc(S("pages_in"), 16)
            nc.gpsimd.memset(zt[:, :, :], 0.0).then_inc(S("zt"), 1)
            nc.gpsimd.memset(Kbd[:, :, :, :], 0.0).then_inc(S("Kbd0"), 1)
            e.wait_ge(S("s_prm"), 1)
            e.wait_ge(S("cc"), 1)
            for k in range(2):
                gs = slice(GH * k, GH * k + GH)
                sh = [P, GH, T + 1, GC]
                pr, pi = (P9[:, :, i, gs].rearrange("p t g -> p g t").unsqueeze(3).to_broadcast(sh) for i in (0, 1))
                cr, ci = (cc[:, i, gs, :].unsqueeze(2).to_broadcast(sh) for i in (0, 1))
                nc.gpsimd.tensor_tensor(Y[1][:, gs, :, :], ci, pr, ALU.mult)
                own(nc.gpsimd.tensor_tensor(ytmp[1][:, :, :, :], cr, pi, ALU.mult))
                nc.gpsimd.tensor_tensor(Y[1][:, gs, :, :], Y[1][:, gs, :, :], ytmp[1][:, :, :, :],
                                        ALU.subtract).then_inc(S("Y_im"), 1)
                e.wait_ge(S("Y_im"), k + 1)
            for b in range(NX):
                if b >= 2:
                    e.wait_ge(S("X_t"), b - 1)
                x_part(e, own, nc.gpsimd, xtmp2, b, 1).then_inc(S("X_im"), 1)
            e.wait_ge(S("K_acc"), 8)
            e.wait_ge(S("k_out"), 32)
            nc.gpsimd.memset(Hz[:, :, :, :, :], 0.0).then_inc(S("Hz0"), 1)
            e.wait_ge(S("wrep"), 128)
            for g in range(G):
                if g >= 2:
                    e.wait_ge(S("bd_used"), g - 1)
                nc.gpsimd.tensor_tensor(
                    bd[g % 2][:, :, :, :],
                    wrep[:, g, :].rearrange("p (h e) -> p h e", h=2).unsqueeze(2).to_broadcast([P, 2, T, GC]),
                    m8[:, :].unsqueeze(1).unsqueeze(3).to_broadcast([P, 2, T, GC]), ALU.mult).then_inc(S("bd"), 1)

        def x_part(e, own, eng, tmp, b, i):
            gs = slice(2 * b, 2 * b + 2)
            sh = [P, 2, T, GC]
            pr, pi = (PR[:, k, gs, :].unsqueeze(3).to_broadcast(sh) for k in (0, 1))
            br, bi = (bb[:, k, gs, :].unsqueeze(2).to_broadcast(sh) for k in (0, 1))
            x = Xn[b % 2][:, i, :, :, :]
            if b:
                e.wait_ge(S(("X_re", "X_im")[i]), b)
            eng.tensor_tensor(x, pr, (br, bi)[i], ALU.mult)
            own(eng.tensor_tensor(tmp[:, :, :, :], pi, (bi, br)[i], ALU.mult))
            return eng.tensor_tensor(x, x, tmp[:, :, :, :], (ALU.subtract, ALU.add)[i])

        def series(own, p, x, inv):
            own(nc.vector.tensor_scalar(p, x, 1.0 / inv[0], None, ALU.mult))
            for c in inv[1:]:
                own(nc.vector.scalar_tensor_tensor(p, p, 1.0 / c, x, ALU.add, ALU.mult))

        def exp_to(own, out, x):
            V = nc.vector
            n, r, q = (Sj[:, j, 0, :] for j in range(3))
            own(V.tensor_scalar(n, x, 1.0 / math.log(2.0), MAGIC, ALU.mult, ALU.add))
            own(V.tensor_scalar(n, n, -MAGIC, None, ALU.add))
            own(V.scalar_tensor_tensor(r, n, -LN1, x, ALU.mult, ALU.add))
            own(V.scalar_tensor_tensor(r, n, -LN2, r, ALU.mult, ALU.add))
            series(own, q, r, [math.factorial(k) for k in (8, 7, 6, 5, 4, 3, 2, 1)])
            own(V.tensor_scalar(n, n, -126.0, 127.0, ALU.max, ALU.min))
            own(V.tensor_scalar(expi[:, :], n, 2.0 ** 23, 127.0 * 2.0 ** 23, ALU.mult, ALU.add))
            own(V.scalar_tensor_tensor(out, q, 1.0, expi[:, :].bitcast(F32), ALU.add, ALU.mult))

        (LDT, ARE, AIM, ARD, ANG, MAG, RED, K0, SIN, COS, DEN, NR_, KRE, KIM, T1, T2) = (
            prm[:, i, :] for i in range(16))
        LR, LI = P9[:, 1, 0, :], P9[:, 1, 1, :]
        V = nc.vector

        def prm_rows(e):
            e.wait_ge(S("prm_T"), 1)
            nc.vector.tensor_copy(LDT[0:64], ps[0][0:64, 64:128].rearrange("p (g r) -> p g r", r=2)[:, :, 0])
            nc.vector.tensor_copy(LDT[64:128], ps[0][64:128, 64:128].rearrange("p (g r) -> p g r", r=2)[:, :, 1])
            nc.vector.tensor_copy(ARE, ps[0][:, 0:32])
            nc.vector.tensor_copy(AIM, ps[0][:, 32:64])
            nc.vector.tensor_copy(bgT[:, :, :], ps[0][:, 128:256].rearrange("p (h g) -> p h g", h=2))
            nc.vector.tensor_copy(d32[:, :], ps[0][0:32, 256:288]).then_inc(S("prm_ev"), 1)

        def prm_exp(e, own):
            e.wait_ge(S("prm_ev"), 1)
            exp_to(own, LDT, LDT)
            own(V.tensor_tensor(ARD, ARE, LDT, ALU.mult))
            own(V.tensor_tensor(ANG, AIM, LDT, ALU.mult))
            exp_to(own, MAG, ARD)

        def prm_angle(e, own):
            own(V.tensor_scalar(K0, ANG, 1.0 / (2.0 * math.pi), MAGIC, ALU.mult, ALU.add))
            own(V.tensor_scalar(K0, K0, -MAGIC, None, ALU.add))
            own(V.scalar_tensor_tensor(RED, K0, -TP1, ANG, ALU.mult, ALU.add))
            own(V.scalar_tensor_tensor(RED, K0, -TP2, RED, ALU.mult, ALU.add))
            own(V.scalar_tensor_tensor(RED, K0, -TP3, RED, ALU.mult, ALU.add))
            own(V.tensor_scalar(RED, RED, 0.25, None, ALU.mult))
            own(V.tensor_tensor(T1, RED, RED, ALU.mult))
            series(own, SIN, T1, [math.factorial(2 * k + 1) * (-1.0) ** k for k in (4, 3, 2, 1)])
            own(V.scalar_tensor_tensor(SIN, SIN, 1.0, RED, ALU.add, ALU.mult))
            series(own, COS, T1, [-math.factorial(2 * k) * (-1.0) ** k for k in (5, 4, 3, 2, 1)])
            for k in range(2):
                own(V.tensor_scalar(COS, COS, -2.0, 2.0, ALU.mult, ALU.add))
                own(V.tensor_tensor(T1, SIN, SIN, ALU.mult))
                own(V.tensor_tensor(SIN, SIN, COS, ALU.mult))
                own(V.tensor_scalar(COS, T1, 2.0, None, ALU.mult))
            own(V.tensor_scalar(COS, COS, -1.0, 1.0, ALU.mult, ALU.add))

        def prm_gain(e, own):
            own(V.tensor_tensor(DEN, ARE, ARE, ALU.mult))
            own(V.tensor_tensor(T2, AIM, AIM, ALU.mult))
            own(V.tensor_tensor(DEN, DEN, T2, ALU.add))
            own(V.reciprocal(DEN, DEN))
            own(V.memset(P9[:, 0, 0, :], 1.0))
            own(V.memset(P9[:, 0, 1, :], 0.0))
            own(V.tensor_tensor(LR, MAG, COS, ALU.mult))
            own(V.tensor_tensor(LI, MAG, SIN, ALU.mult))
            own(V.tensor_scalar(NR_, LR, -1.0, None, ALU.add))
            own(V.tensor_tensor(KRE, NR_, ARE, ALU.mult))
            own(V.tensor_tensor(T2, LI, AIM, ALU.mult))
            own(V.tensor_tensor(KRE, KRE, T2, ALU.add))
            own(V.tensor_tensor(KRE, KRE, DEN, ALU.mult))
            own(V.tensor_tensor(KIM, LI, ARE, ALU.mult))
            own(V.tensor_tensor(T2, NR_, AIM, ALU.mult))
            own(V.tensor_tensor(KIM, KIM, T2, ALU.subtract))
            own(V.tensor_tensor(KIM, KIM, DEN, ALU.mult))

        def prm_powers(e, own):
            for k in range(2, T + 1):
                sh = [P, 2, GP]
                V.tensor_tensor(rt[:, 0], P9[:, k - 1], LR.unsqueeze(1).to_broadcast(sh), ALU.mult)
                own(V.tensor_tensor(rt[:, 1], P9[:, k - 1], LI.unsqueeze(1).to_broadcast(sh), ALU.mult))
                V.tensor_tensor(P9[:, k, 0], rt[:, 0, 0], rt[:, 1, 1], ALU.subtract)
                own(V.tensor_tensor(P9[:, k, 1], rt[:, 0, 1], rt[:, 1, 0], ALU.add))

        def s_dve(e):
            own = owns["dve"]
            p_done(e)
            V = nc.vector
            KRE, KIM = prm[:, 12, :], prm[:, 13, :]
            e.wait_ge(S("prm_T"), 2)
            nc.vector.tensor_copy(h0[:, :, :, :].rearrange("p i b g -> p (i b g)"), ps[1][:, :]).then_inc(
                S("prm_ev"), 1)
            e.wait_ge(S("prm_ev"), 2)
            for s in range(T):
                ins = V.tensor_copy(PR[:, :, :, s], P9[:, T - 1 - s])
            own(ins)
            e.wait_ge(S("bt_in"), 32)
            sh = [P, GP, GC]
            kr, ki = (x.unsqueeze(2).to_broadcast(sh) for x in (KRE, KIM))
            t512 = Sj[:, 0:8, :, :].rearrange("p a b c -> p (a b c)").rearrange("p (g c) -> p g c", g=GP)
            for (dst, x1, x2, op) in ((0, 0, 1, ALU.subtract), (1, 1, 0, ALU.add)):
                own(V.tensor_tensor(bb[:, dst], kr, bt[:, x1], ALU.mult))
                own(V.tensor_tensor(t512, ki, bt[:, x2], ALU.mult))
                own(V.tensor_tensor(bb[:, dst], bb[:, dst], t512, op))
            e.wait_ge(S("c_T"), 1)
            own(V.tensor_copy(cc[:, 0], ps[2][:, :].rearrange("p (g c) -> p g c", g=GP)))
            V.tensor_scalar(cc[:, 1], ps[3][:, :].rearrange("p (g c) -> p g c", g=GP), -1.0, None, ALU.mult).then_inc(
                S("cc"), 1)
            e.wait_ge(S("cc"), 1)
            e.wait_ge(S("Kbd0"), 1)
            for r in range(2):
                ins = V.tensor_copy(Kbd[r * 64:r * 64 + 64, :, :, r * GC:r * GC + GC], bb[r * 64:r * 64 + 64])
            ins.then_inc(S("Kbd"), 1)
            V.tensor_copy(dT[:, 0:1], d32[:, 0:1]).then_inc(S("s_prm"), 1)
            for k in range(2):
                gs = slice(GH * k, GH * k + GH)
                sh = [P, GH, T + 1, GC]
                pr, pi = (P9[:, :, i, gs].rearrange("p t g -> p g t").unsqueeze(3).to_broadcast(sh) for i in (0, 1))
                cr, ci = (cc[:, i, gs, :].unsqueeze(2).to_broadcast(sh) for i in (0, 1))
                V.tensor_tensor(Y[0][:, gs, :, :], cr, pr, ALU.mult)
                own(V.tensor_tensor(ytmp[0][:, :, :, :], ci, pi, ALU.mult))
                ins = V.tensor_tensor(Y[0][:, gs, :, :], Y[0][:, gs, :, :], ytmp[0][:, :, :, :], ALU.add)
                if k == 0:
                    own(ins)
            ins.then_inc(S("Y_re"), 1)
            e.wait_ge(S("Y_re"), 1)
            e.wait_ge(S("Y_im"), 2)

            def xs(b):
                if b >= 2:
                    e.wait_ge(S("X_t"), b - 1)
                x_part(e, own, V, xtmp, b, 0).then_inc(S("X_re"), 1)

            xs(0)
            xs(1)
            for b in range(8):
                e.wait_ge(S("K_acc"), b + 1)
                own(V.tensor_copy(Kst[:, 4 * b:4 * b + 4, :],
                                  ps[4 + b % 2][0:32, :].rearrange("p (q w) -> p q w", q=4)))
                for q in range(4):
                    gp = 4 * b + q
                    ins = V.scalar_tensor_tensor(Kst[:, gp, 0:GC], eye16[:, :], d32[:, gp:gp + 1],
                                                 Kst[:, gp, 0:GC], ALU.mult, ALU.add)
                ins.then_inc(S("K_ev"), 1)
            for b in range(NX):
                if 1 < b + 1 < NX:
                    xs(b + 1)
                e.wait_ge(S("s_acc"), b + 1)
                V.tensor_copy(Sj[:, :, :, 2 * b:2 * b + 2].rearrange("p j i q -> p q i j"),
                              ps[b % 2][:, 0:4 * NJ].rearrange("p (q i j) -> p q i j", q=2, i=2)).then_inc(
                    S("S_ev"), 1)
            e.wait_ge(S("S_ev"), NX)
            own(V.memset(Hst[:, 0, :, :], 0.0))
            sh = [P, 2, GP]
            l8r, l8i = (P9[:, T, i, :].unsqueeze(1).to_broadcast(sh) for i in (0, 1))
            V.tensor_tensor(rt[:, 0], P9[:, T], l8r, ALU.mult)
            own(V.tensor_tensor(rt[:, 1], P9[:, T], l8i, ALU.mult))
            V.tensor_tensor(L16[:, 0], rt[:, 0, 0], rt[:, 1, 1], ALU.subtract)
            own(V.tensor_tensor(L16[:, 1], rt[:, 0, 1], rt[:, 1, 0], ALU.add))
            HC = NCH // 2
            ev, od = (Sj[:, 0:NCH].rearrange("p (a b) i g -> p a b i g", b=2)[:, :, b] for b in (0, 1))
            full = [P, HC, GP]
            f8r, f8i = (P9[:, T, i, :].unsqueeze(1).to_broadcast(full) for i in (0, 1))
            tmp = Hst[:, 33:33 + HC]
            for i in (0, 1):
                ins = V.tensor_tensor(tmp[:, :, i], ev[:, :, i], f8r, ALU.mult)
            own(ins)
            own(V.tensor_tensor(od, od, tmp, ALU.add))
            for i in (0, 1):
                ins = V.tensor_tensor(tmp[:, :, i], ev[:, :, 1 - i], f8i, ALU.mult)
            own(ins)
            V.tensor_tensor(od[:, :, 0], od[:, :, 0], tmp[:, :, 0], ALU.subtract)
            own(V.tensor_tensor(od[:, :, 1], od[:, :, 1], tmp[:, :, 1], ALU.add))
            l16r, l16i = (L16[:, i].unsqueeze(1).to_broadcast(sh) for i in (0, 1))
            for j in range(0, NCH, 2):
                V.tensor_tensor(rt[:, 0], Hst[:, j], l16r, ALU.mult)
                own(V.tensor_tensor(rt[:, 1], Hst[:, j], l16i, ALU.mult))
                own(V.tensor_tensor(rt[:, 0], rt[:, 0], Sj[:, j + 1], ALU.add))
                V.tensor_tensor(Hst[:, j + 2, 0], rt[:, 0, 0], rt[:, 1, 1], ALU.subtract)
                own(V.tensor_tensor(Hst[:, j + 2, 1], rt[:, 0, 1], rt[:, 1, 0], ALU.add))
            he, ho = (Hst[:, 0:NCH].rearrange("p (a b) i g -> p a b i g", b=2)[:, :, b] for b in (0, 1))
            for i in (0, 1):
                V.tensor_tensor(ho[:, :, i], he[:, :, i], f8r, ALU.mult)
                ins = V.tensor_tensor(od[:, :, i], he[:, :, 1 - i], f8i, ALU.mult)
            own(ins)
            own(V.tensor_tensor(ho, ho, ev, ALU.add))
            V.tensor_tensor(ho[:, :, 0], ho[:, :, 0], od[:, :, 0], ALU.subtract)
            own(V.tensor_tensor(ho[:, :, 1], ho[:, :, 1], od[:, :, 1], ALU.add))
            l8r, l8i = (P9[:, T, i, :].unsqueeze(1).to_broadcast([P, NB, GP]) for i in (0, 1))
            for i in range(2):
                own(V.tensor_tensor(hs[:, i], h0[:, i], l8r, ALU.mult))
            own(V.tensor_tensor(hs[:, 0], hs[:, 0], Sj[:, NCH:NJ, 0, :], ALU.add))
            own(V.tensor_tensor(hs[:, 1], hs[:, 1], Sj[:, NCH:NJ, 1, :], ALU.add))
            hw = prm[:, 0:8, :]
            own(V.tensor_tensor(hw, h0[:, 1], l8i, ALU.mult))
            own(V.tensor_tensor(hs[:, 0], hs[:, 0], hw, ALU.subtract))
            own(V.tensor_tensor(hw, h0[:, 0], l8i, ALU.mult))
            V.tensor_tensor(hs[:, 1], hs[:, 1], hw, ALU.add).then_inc(S("hs"), 1)
            e.wait_ge(S("Hz0"), 1)
            for i in range(2):
                for r in range(2):
                    rp = slice(r * 64, r * 64 + 64)
                    ins = V.tensor_copy(Hz[rp, :, i, r, NCH:NJ], h0[rp, i].rearrange("p b g -> p g b"))
                    if i == 0:
                        ins = V.tensor_copy(Hz[rp, :, i, r, 0:NCH], Hst[rp, 0:NCH, i, :].rearrange("p j g -> p g j"))
                if i == 0:
                    ins.then_inc(S("Hz_a"), 1)
            ins.then_inc(S("Hz"), 1)
            e.wait_ge(S("h_T"), 1)
            e.wait_ge(S("y_acc"), 16)
            V.tensor_copy(hout[:, :, 0:2, :], ps[0][:, :].rearrange("p (i k n) -> p i k n", i=2, k=2)).then_inc(
                S("h_out"), 1)
            V.tensor_copy(hout[0:GP, :, 2, :], ps[1][0:GP, 0:2 * P].rearrange("p (i n) -> p i n", i=2)).then_inc(
                S("h_out"), 2)
            e.wait_ge(S("gelu"), 16)
            sh = [P, 4, NJ]
            for b in range(16):
                bv, bg = (bgT[:, i, 4 * b:4 * b + 4].unsqueeze(2).to_broadcast(sh) for i in (0, 1))
                e.wait_ge(S("bd_used"), 4 * b + 4)
                pv, pg = (ps[2 + 2 * (b % 3) + i][:, 0:4 * NJ].rearrange("p (g j) -> p g j", g=4) for i in (0, 1))
                if b >= 2:
                    e.wait_ge(S("glu"), b - 1)
                V.tensor_tensor(gl2[b % 2][:, :, :], pg, bg, ALU.add).then_inc(S("gl_g"), 1)
                own(V.tensor_tensor(gl1[b % 2][:, :, :], pv, bv, ALU.add))
                e.wait_ge(S("sig"), b + 1)
                V.tensor_tensor(Zo[:, 4 * b:4 * b + 4, :], gl1[b % 2][:, :, :], gl2[b % 2][:, :, :],
                                ALU.mult).then_inc(S("glu"), 1)

        def s_act(e):
            p_done(e)
            for b in range(NX):
                e.wait_ge(S("X_t"), b + 1)
                if b >= 2:
                    e.wait_ge(S("s_acc"), b - 1)
                nc.scalar.activation(XT[b % 2][:, :, :], ps[6 + b % 2][:, :].rearrange("p (q n) -> p q n", q=4),
                                     ACT.Copy).then_inc(S("X_T"), 1)
            e.wait_ge(S("hs"), 1)
            e.wait_ge(S("Hz0"), 1)
            for r in range(2):
                rp = slice(r * 64, r * 64 + 64)
                nc.scalar.activation(Hz[rp, :, 1, r, 0:NCH], Hst[rp, 0:NCH, 1, :].rearrange("p j g -> p g j"),
                                     ACT.Copy).then_inc(S("Hz"), 1)
            for b in range(16):
                e.wait_ge(S("y_acc"), b + 1)
                nc.scalar.activation(Z[:, 4 * b:4 * b + 4, :], ps[2 + b % 4][:, 0:4 * NJ].rearrange(
                    "p (g j) -> p g j", g=4), ACT.Gelu_apprx_tanh).then_inc(S("gelu"), 1)
            for b in range(16):
                e.wait_ge(S("gl_g"), b + 1)
                nc.scalar.activation(gl2[b % 2][:, :, :], gl2[b % 2][:, :, :], ACT.Sigmoid).then_inc(S("sig"), 1)

        NPOOL = a["cache_k"].shape[1]
        RING = 12
        KTB = [0, 1, 5, 6]
        PTB = [7, 5]
        KG = PAST // 512
        NG = NB * KG
        d_d = scratch("d_d", (NB * PAGES, H, PAGE))
        pg = [at(f"pg{i}", [P, AW], W0 + 4096 * i) for i in range(RING)]
        KT = [at(f"KT{i}", [P, H, 512], W0 + 49152 + 16384 * i) for i in range(2)]
        lfr = at("lfr", [P, PAGE, H], W0 + 65536)
        pre = at("pre", [P, H, PAGE], W0 + 69632)
        one = at("one", [P, PAGE], W0 + 73728)
        sc = [at(f"sc{i}", [P, 2, PAST + NQ], W0 + 81920 + 16448 * i) for i in range(2)]
        DZ = W0 + 114816
        PT = [at(f"PT{i}", [P, 2, 4, NQ], DZ + 256 * i) for i in range(4)]
        sel = at("sel", [H, 2, P], DZ + 1024, F32R)
        outO = at("outO", [P, 2, P], DZ + 2048)
        cm8 = at("cm8", [P, NQ], DZ + 3072)
        mxs = at("mxs", [P, 2, KG + 1], DZ + 3104)
        nmx = at("nmx", [P, 2, 2], DZ + 3168)
        lsum = at("lsum", [P, 2, 2], DZ + 3200)
        rec = at("rec", [P, 2], DZ + 3232)
        totl = at("totl", [P, H], DZ + 3264)
        offs = at("offs", [P, H], DZ + 3296)
        draw = at("draw", [H, PAST], R0 + 34816)
        dhi = at("dhi", [H, PAST], R0 + 43008, F32R)
        dlo = at("dlo", [H, PAST], R0 + 51200, F32R)
        mixO = at("mixO", [P, H, NS], R0 + 59392)

        def s_done(e):
            e.wait_ge(S("glu"), 16)
            e.wait_ge(S("st_out"), 96)

        def page_list():
            keys = lambda i: [("cache_k", i // KG, i % KG * 4 + k, ("kturn_d", H * i + H)) for k in range(4)]
            values = lambda b: [("cache_v", b, k, ("page_used", 17 * b + k + 1)) for k in range(PAGES + 1)]
            out = []
            for i in range(NG):
                out += keys(i)
                if i % KG == 0 and i >= 2 * KG:
                    out += values(i // KG - 2)
            return out + values(NB - 2) + values(NB - 1)

        def cache_pages(e, ns):
            loads = page_list()
            e.wait_ge(S("pages_in"), 16)
            for n in ns:
                cache, b, k, _ = loads[n]
                if n >= RING:
                    name, count = loads[n - RING][3]
                    e.wait_ge(S(name), B(name) + count)
                if k < PAGES:
                    c = b * PAGES + k
                    r = e.value_load(pages[0:1, c:c + 1], min_val=0, max_val=NPOOL - 1)
                    dst, src = pg[n % RING][:, :], a[cache][0][bass.ds(r, 1)].rearrange("o p h d -> (o p) (h d)")
                else:
                    dst, src = pg[n % RING][0:NQ, :], o["v_sample"][0, b].rearrange("q h d -> q (h d)")
                e.dma_start(dst, src).then_inc(S(f"page{n % RING}"), 16)

        def d_sp(e):
            s_done(e)
            e.wait_ge(S("bd_used"), G)
            cache_pages(e, range(9, len(page_list())))

        def d_pool(e):
            own = owns["pool"]
            s_done(e)
            e.wait_ge(S("pageid"), 16)
            e.indirect_dma_start(lfr[:, :, :].rearrange("p s h -> p (s h)"), None,
                                 a["cache_logf"][0].rearrange("n s h -> n (s h)"),
                                 bass.IndirectOffsetOnAxis(ap=pageid[:, 0:1], axis=0)).then_inc(S("lf_in"), 16)
            nc.gpsimd.memset(one[:, :], 1.0)
            for half in range(2):
                own(nc.gpsimd.tensor_copy(
                    sel[:, half, :].rearrange("h (j x) -> h j x", j=4),
                    ident[0:H, 4 * half:4 * half + 4].unsqueeze(2).to_broadcast([H, 4, 32])))
            own(nc.gpsimd.memset(outO[:, 0, :], 0.0))
            cw = outO[:, 0, 0:32].rearrange("p (j t) -> p j t", j=4)
            own(nc.gpsimd.affine_select(out=cw, in_=cw, compare_op=ALU.is_ge, fill=NEG, base=0,
                                        pattern=[[-32, 4], [-1, NQ]], channel_multiplier=1))
            own(nc.gpsimd.affine_select(out=cw, in_=cw, compare_op=ALU.is_ge, fill=0.0, base=31,
                                        pattern=[[32, 4], [0, NQ]], channel_multiplier=-1))
            own(nc.gpsimd.affine_select(out=cw, in_=cw, compare_op=ALU.is_ge, fill=0.0, base=0,
                                        pattern=[[-32, 4], [0, NQ]], channel_multiplier=1))
            own(nc.gpsimd.tensor_tensor(cm8[:, :], cw[:, 0, :], cw[:, 1, :], ALU.add))
            own(nc.gpsimd.tensor_tensor(cm8[:, :], cm8[:, :], cw[:, 2, :], ALU.add))
            nc.gpsimd.tensor_tensor(cm8[:, :], cm8[:, :], cw[:, 3, :], ALU.add).then_inc(S("d_const"), 1)
            e.wait_ge(S("D"), B("D") + 1)
            e.dma_start(d_d[:, :, :], pre[:, :, :]).then_inc(S("D_out"), 16)
            e.wait_ge(S("D_out"), B("D_out") + 16)
            for b in range(NB):
                if b:
                    e.wait_ge(S("d_lo"), b)
                e.dma_start(draw[:, :].rearrange("h (k s) -> h k s", k=PAGES),
                            d_d[b * PAGES:b * PAGES + PAGES].rearrange("k h s -> h k s")).then_inc(S("d_in"), 16)
                e.wait_ge(S("d_in"), 16 * b + 16)
                if b:
                    e.wait_ge(S("s_done"), B("s_done") + KG * b)
                own(nc.gpsimd.tensor_copy(dhi[:, :], draw[:, :]))
                nc.gpsimd.tensor_tensor(dlo[:, :], draw[:, :], dhi[:, :].bitcast(F32), ALU.subtract).then_inc(
                    S("d_lo"), 1)

        def d_pe(e):
            s_done(e)
            e.wait_ge(S("d_const"), B("d_const") + 1)
            e.wait_ge(S("glu"), 16)
            n = [0]

            def slots(count):
                r = range(n[0], n[0] + count)
                n[0] += count
                return r

            def turn(i, pages_):
                for x in pages_:
                    e.wait_ge(S(f"page{x % RING}"), B(f"page{x % RING}") + 16 * (x // RING) + 16)
                for h in range(H):
                    m = 4 * i + h // 2
                    if m >= 2:
                        e.wait_ge(S(("kt_a", "kt_v")[h % 2]), B("kt_a") + m - 1)
                    for k, x in enumerate(pages_):
                        mm = nc.tensor.transpose(ps[KTB[h % 4]][:, k * P:k * P + P], pg[x % RING][:, h * DH:h * DH + DH],
                                                 ident[:, :])
                    mm.then_inc(S("kturn_d"), 1)

            def score(i):
                b = i // KG
                e.wait_ge(S("kt_a"), B("kt_a") + 4 * i + 4)
                e.wait_ge(S("kt_v"), B("kt_v") + 4 * i + 4)
                if i:
                    e.wait_ge(S("s_cp"), B("s_cp") + 2 * i)
                e.wait_ge(S("d_lo"), b + 1)
                cols = slice(i % KG * 512, i % KG * 512 + 512)
                for half in range(2):
                    acc = ps[3 + half]
                    nc.tensor.matmul(acc[:, :], sel[:, half, :], dhi[:, cols], start=True, stop=False)
                    nc.tensor.matmul(acc[:, :], sel[:, half, :], dlo[:, cols], start=False, stop=True)
                    for j in range(4):
                        h = 4 * half + j
                        mm = nc.tensor.matmul(acc[32 * j:32 * j + NQ, :], qTs[:, h, b * NQ:b * NQ + NQ],
                                              KT[i % 2][:, h, :], start=False, stop=True, skip_group_check=True)
                mm.then_inc(S("s_done"), 1)
                if i % KG == KG - 1:
                    if b:
                        e.wait_ge(S("n_ev"), B("n_ev") + b)
                    for half in range(2):
                        acc = ps[2][:, 256 + 8 * half:264 + 8 * half]
                        cols = slice(b * NQ, b * NQ + NQ)
                        nc.tensor.matmul(acc, sel[:, half, :].bitcast(F32), nfc[:, SEQ + b * NQ:SEQ + b * NQ + NQ],
                                         start=True, stop=True, skip_group_check=True)
                        for j in range(4):
                            h = 4 * half + j
                            mm = nc.tensor.matmul(acc[32 * j:32 * j + NQ, :], qTs[:, h, cols], kTs[:, h, cols],
                                                  start=False, stop=True, skip_group_check=True)
                    mm.then_inc(S("n_acc"), 1)

            def values(b, xs):
                e.wait_ge(S("exp"), B("exp") + 2 * b + 2)
                if b:
                    e.wait_ge(S("o_n"), B("o_n") + b)
                e.wait_ge(S("z2"), B("z2") + 1)
                last = min(b + 2, NB)
                e.wait_ge(S("n_ev"), B("n_ev") + last)
                e.wait_ge(S("kt_a"), B("kt_a") + min(4 * KG * last + 4, 4 * NG))

                def turn_p(k):
                    m = 17 * b + k
                    rows = P if k < PAGES else NQ
                    if m >= 2:
                        e.wait_ge(S("pt_ev"), B("pt_ev") + m - 1)
                    for half in range(2):
                        c = half * P
                        mm = nc.tensor.transpose(ps[PTB[m % 2]][0:rows, c:c + P], sc[b % 2][:, half, k * P:k * P + rows],
                                                 ident[:, :])
                    mm.then_inc(S("pt_t"), 1)

                turn_p(0)
                for k in range(PAGES + 1):
                    m, x = 17 * b + k, xs[k]
                    rows = P if k < PAGES else NQ
                    if k < PAGES:
                        turn_p(k + 1)
                    e.wait_ge(S("pt_ev"), B("pt_ev") + m + 1)
                    e.wait_ge(S(f"page{x % RING}"), B(f"page{x % RING}") + 16 * (x // RING) + 16)
                    for half in range(2):
                        for j in range(4):
                            h = 4 * half + j
                            mm = nc.tensor.matmul(ps[2][32 * j:32 * j + NQ, half * P:half * P + P],
                                                  PT[m % 4][0:rows, half, j, :],
                                                  pg[x % RING][0:rows, h * DH:h * DH + DH], start=k == 0,
                                                  stop=k == PAGES, skip_group_check=True)
                    mm.then_inc(S("page_used"), 1)
                e.wait_ge(S("o_n"), B("o_n") + b + 1)
                for half in range(2):
                    mm = nc.tensor.transpose(ps[7][:, half * P:half * P + P], outO[:, half, :], ident[:, :])
                mm.then_inc(S("o_T"), 1)
                e.wait_ge(S("o_ev"), B("o_ev") + b + 1)

            order = {}
            vslots = {}
            for i in range(NG):
                order[i] = slots(4)
                if i % KG == 0 and i >= 2 * KG:
                    vslots[i // KG - 2] = slots(PAGES + 1)
            vslots[NB - 2] = slots(PAGES + 1)
            vslots[NB - 1] = slots(PAGES + 1)
            turn(0, order[0])
            e.wait_ge(S("totl"), B("totl") + 1)
            nc.tensor.matmul(ps[7][:, 0:H], later[:, :], totl[:, :], start=True, stop=True).then_inc(S("offs"), 1)
            e.wait_ge(S("D"), B("D") + 1)
            for i in range(NG):
                if i + 1 < NG:
                    turn(i + 1, order[i + 1])
                score(i)
                if i % KG == KG - 1 and i >= 2 * KG - 1:
                    values(i // KG - 1, vslots[i // KG - 1])
            values(NB - 1, vslots[NB - 1])

        def kt_evac(e, i, odd):
            if i >= 2:
                e.wait_ge(S("s_done"), B("s_done") + i - 1)
            for h in range(odd, H, 2):
                e.wait_ge(S("kturn_d"), B("kturn_d") + H * i + h + 1)
                if odd:
                    nc.vector.tensor_copy(KT[i % 2][:, h, :], ps[KTB[h % 4]][:, :]).then_inc(S("kt_v"), 1)
                else:
                    nc.scalar.activation(KT[i % 2][:, h, :], ps[KTB[h % 4]][:, :], ACT.Copy).then_inc(S("kt_a"), 1)

        def d_act(e):
            s_done(e)
            kt_evac(e, 0, 0)
            e.wait_ge(S("D_out"), B("D_out") + 16)
            e.wait_ge(S("z_out"), 128)
            for i in range(NG):
                b = i // KG
                if i + 1 < NG:
                    kt_evac(e, i + 1, 0)
                e.wait_ge(S("s_done"), B("s_done") + i + 1)
                if b >= 2:
                    e.wait_ge(S("pt_t"), B("pt_t") + 17 * (b - 1))
                for half in range(2):
                    nc.scalar.activation(sc[b % 2][:, half, i % KG * 512:i % KG * 512 + 512],
                                         ps[3 + half][:, :], ACT.Copy).then_inc(S("s_cp"), 1)
                if i % KG == KG - 1:
                    e.wait_ge(S("s_cp"), B("s_cp") + 2 * i + 2)
                    e.wait_ge(S("mx"), B("mx") + b + 1)
                    for half in range(2):
                        nc.scalar.activation(sc[b % 2][:, half, :], sc[b % 2][:, half, :], ACT.Exp,
                                             bias=nmx[:, b % 2, half:half + 1],
                                             accum_out=lsum[:, b % 2, half:half + 1]).then_inc(S("exp"), 1)
            e.wait_ge(S("zr_in"), 16)
            mix_high(e, range(4))

        def d_dve(e):
            own = owns["dve"]
            V = nc.vector
            s_done(e)
            kt_evac(e, 0, 1)
            e.wait_ge(S("lf_in"), 16)
            e.wait_ge(S("d_const"), B("d_const") + 1)
            for h in range(H):
                own(V.tensor_tensor_scan(pre[:, h, :], one[:, :], lfr[:, :, h], 0.0, ALU.mult, ALU.add))
            V.tensor_copy(totl[:, :], pre[:, :, PAGE - 1]).then_inc(S("totl"), 1)
            e.wait_ge(S("gelu"), 16)
            V.memset(ps[2][:, 0:256], 0.0).then_inc(S("z2"), 1)
            e.wait_ge(S("offs"), B("offs") + 1)
            own(V.tensor_copy(offs[:, :], ps[7][:, 0:H]))
            V.tensor_tensor(pre[:, :, :], offs[:, :].unsqueeze(2).to_broadcast([P, H, PAGE]), pre[:, :, :],
                            ALU.subtract).then_inc(S("D"), 1)
            e.wait_ge(S("D_out"), B("D_out") + 16)

            def values(b):
                for k in range(PAGES + 1):
                    m = 17 * b + k
                    rows = P if k < PAGES else NQ
                    e.wait_ge(S("pt_t"), B("pt_t") + m + 1)
                    if m >= 4:
                        e.wait_ge(S("page_used"), B("page_used") + m - 3)
                    V.tensor_copy(PT[m % 4][0:rows, :, :, :].rearrange("p a j q -> p (a j) q"),
                                  ps[PTB[m % 2]][0:rows, 0:256].rearrange(
                                      "p (a x) -> p a x", x=32)[:, :, 0:NQ]).then_inc(S("pt_ev"), 1)
                own(V.reciprocal(rec[:, :], lsum[:, b % 2, :]))
                e.wait_ge(S("page_used"), B("page_used") + 17 * b + 17)
                for half in range(2):
                    ins = V.tensor_scalar(outO[:, half, :], ps[2][:, half * P:half * P + P], rec[:, half:half + 1],
                                          None, ALU.mult)
                ins.then_inc(S("o_n"), 1)
                e.wait_ge(S("o_T"), B("o_T") + b + 1)
                V.tensor_copy(mixO[:, :, b * NQ:b * NQ + NQ],
                              ps[7][:, 0:256].rearrange("p (a x) -> p a x", x=32)[:, :, 0:NQ]).then_inc(S("o_ev"), 1)

            for i in range(NG):
                b = i // KG
                if i + 1 < NG:
                    kt_evac(e, i + 1, 1)
                e.wait_ge(S("s_cp"), B("s_cp") + 2 * i + 2)
                if i % KG == 0 and b:
                    e.wait_ge(S("mx"), B("mx") + b)
                V.tensor_reduce(mxs[:, :, i % KG], sc[b % 2][:, :, i % KG * 512:i % KG * 512 + 512], AX.X,
                                ALU.max).then_inc(S("s_mx"), 1)
                if i % KG == KG - 1:
                    e.wait_ge(S("n_acc"), B("n_acc") + b + 1)
                    if b >= 2:
                        e.wait_ge(S("pt_t"), B("pt_t") + 17 * (b - 1))
                    V.tensor_tensor(sc[b % 2][:, :, PAST:PAST + NQ],
                                    ps[2][:, 256:272].rearrange("p (a t) -> p a t", a=2),
                                    cm8[:, :].unsqueeze(1).to_broadcast([P, 2, NQ]), ALU.add).then_inc(S("n_ev"), 1)
                    e.wait_ge(S("n_ev"), B("n_ev") + b + 1)
                    e.wait_ge(S("s_mx"), B("s_mx") + i + 1)
                    own(V.tensor_reduce(mxs[:, :, KG], sc[b % 2][:, :, PAST:PAST + NQ], AX.X, ALU.max))
                    V.tensor_reduce(nmx[:, b % 2, :], mxs[:, :, :], AX.X, ALU.max, negate=True).then_inc(S("mx"), 1)
                if i % KG == KG - 1 and i >= 2 * KG - 1:
                    e.wait_ge(S("exp"), B("exp") + 2 * (b - 1) + 2)
                    values(b - 1)
            e.wait_ge(S("exp"), B("exp") + 2 * NB)
            values(NB - 1)

        x1_d = scratch("x1_d", (SEQ + NS, D))
        yt = at("yt", [P, TILES, D], R0)
        xr = [[at(f"xr{i}_{t}", [P, CW], R0 + 40960 + 10240 * i + 2048 * t) for t in range(TILES)] for i in range(2)]
        gr = [[at(f"gr{i}_{k}", [P, CW], R0 + 61440 + 4096 * i + 2048 * k) for k in range(2)] for i in range(2)]
        grow = at("grow", [P, D], R0 + 40960)
        brow = at("brow", [P, D], R0 + 49152)
        val2 = [at(f"val2_{i}", [P, CW], R0 + 57344 + 2048 * i) for i in range(2)]
        xn2 = [at(f"xn2_{i}", [P, D], W0 + 16384 + 8192 * i) for i in range(2)]
        rhi = at("rhi", [P, 4, SEQ], R0 + 40960, F32R)
        rlo = at("rlo", [P, 4, SEQ], R0 + 49152, F32R)
        rsm = at("rsm", [P, 4, 2 * NS], R0 + 57344, F32R)
        rv = [at(f"rv{t}", [P, SEQ], R0 + 59392 + 2048 * t) for t in range(4)]
        csm = at("csm", [64, CW], R0 + 67584)
        g2row = [at(f"g2row{k}", [P, D], X0 + 8192 * k) for k in range(2)]
        grow2 = at("grow2", [P, D], X0 + 16384)
        brow2 = at("brow2", [P, D], X0 + 24576)
        x1t = [at(f"x1t{t}", [P, D], X0 + 32768 + 8192 * t) for t in range(TILES)]
        WO = [("o", 8 + n, 64 + 8 * n, 8, n) for n in range(4)]
        FN = []
        NF = FF // CW
        for f in range(NF):
            FN.append(("up", 12 + 5 * f, 96 + 16 * f, 8, f))
            for n in range(4):
                FN.append(("down", 13 + 5 * f + n, 104 + 16 * f + 2 * n, 2, (f, n)))

        def d_done(e):
            e.wait_ge(S("zr_in"), 16)
            e.wait_ge(S("o_ev"), B("o_ev") + NB)
            e.wait_ge(S("d_lo"), NB)

        def weight_src(kind, q, x):
            rows = slice(q * GK * P, (q + 1) * GK * P)
            if kind == "o":
                return a["w_o"][0][rows, x * CW:x * CW + CW]
            if kind == "up":
                return a["w_up"][0][rows, x * CW:x * CW + CW]
            f, n = x
            return a["w_down"][0][f * CW + q * GK * P:f * CW + (q + 1) * GK * P, n * CW:n * CW + CW]

        def f_sp(e):
            d_done(e)
            for kind, c, g0, ng, x in WO + FN:
                for q in range(ng):
                    load_w(e, g0 + q, g0 + q, weight_src(kind, q, x), False)

        def stream(e, split, chunks, evac):
            todo = []
            for ch in chunks:
                for g in range(ch[2], ch[2] + ch[3]):
                    if todo and todo[0][2] + todo[0][3] + LAG - 1 <= g:
                        evac(todo.pop(0))
                    split(g)
                todo.append(ch)
            for ch in todo:
                evac(ch)

        def row_src(t):
            return slice(t * P, t * P + tile_rows(t))

        def f_pool(e):
            own = owns["pool"]
            d_done(e)

            def rows_in(n):
                if n >= 2:
                    e.wait_ge(S("o_row"), n - 1)
                cs = slice(n * CW, n * CW + CW)
                for t in range(TILES):
                    src = x_p[t * P:t * P + P, cs] if t < NT else x_s[:, cs]
                    e.dma_start(xr[n % 2][t][0:tile_rows(t), :], src).then_inc(S(f"row_in{n % 2}"), 16)
                e.dma_start(gr[n % 2][0][:, :], gate_d[0, 0:P, cs]).then_inc(S(f"row_in{n % 2}"), 16)
                e.dma_start(gr[n % 2][1][0:NS, :], gate_d[0, P:P + NS, cs]).then_inc(S(f"row_in{n % 2}"), 16)

            mix_low(e, nc.gpsimd, (2, 3, 5), "mix_lo")
            mix_ready(e)
            for n in range(4):
                rows_in(n)
            e.wait_ge(S("o_row"), 4)
            e.dma_start(grow[:, :], a["ln1_g"].to_broadcast([P, D])).then_inc(S("gb_in"), 16)
            e.dma_start(brow[:, :], a["ln1_b"].to_broadcast([P, D])).then_inc(S("gb_in"), 16)
            for t in range(TILES):
                e.wait_ge(S("x1"), B("x1") + t + 1)
                e.dma_start(x1_d[row_src(t), :], yt[0:tile_rows(t), t, :]).then_inc(S("x1_out"), 16)
                for i, (tt, q) in enumerate(GROUPS):
                    if tt == t:
                        turn_pool(e, "a", i, 1)
            for f in range(NF):
                for t in range(4):
                    e.wait_ge(S("r_hi"), B("r_hi") + 4 * f + t + 1)
                    nc.gpsimd.tensor_tensor(rlo[:, t, :], rv[t][:, :], rhi[:, t, :].bitcast(F32),
                                            ALU.subtract).then_inc(S("r_lo"), 1)
            e.wait_ge(S("w_used"), 96 + 16 * (NF - 1) + 8)
            e.dma_start(g2row[0][:, :], gate_d[1, 0:P, :]).then_inc(S("last_in"), 16)
            e.dma_start(g2row[1][0:NS, :], gate_d[1, P:P + NS, :]).then_inc(S("last_in"), 16)
            e.dma_start(grow2[:, :], a["ln2_g"].to_broadcast([P, D])).then_inc(S("last_in"), 16)
            e.dma_start(brow2[:, :], a["ln2_b"].to_broadcast([P, D])).then_inc(S("last_in"), 16)
            e.wait_ge(S("x1_out"), 16 * TILES)

            for t in range(TILES):
                e.dma_start(x1t[t][0:tile_rows(t), :], x1_d[row_src(t), :]).then_inc(S("last_in"), 16)
            for t in range(TILES):
                e.wait_ge(S("y_row"), B("y_row") + t + 1)
                y = yt[0:tile_rows(t), t, :]
                nc.gpsimd.tensor_tensor(y, y, brow2[0:tile_rows(t), :], ALU.add).then_inc(S("y_out"), 1)
                e.wait_ge(S("y_out"), B("y_out") + t + 1)
                dst = (o["y_prompt"][0, t * P:t * P + P] if t < NT else o["y_sample"].rearrange("b q d -> (b q) d"))
                e.dma_start(dst, yt[0:tile_rows(t), t, :]).then_inc(S("out"), 16)
            e.wait_ge(S("out"), 16 * TILES)

        def mix_part(i, lo):
            if i < 4:
                ks = slice(4 * i, 4 * i + 4)
                dst = (xhi, xlo)[lo][:, ks, :]
                if i < 2:
                    return dst, qT[:, ks, :]
                return (dst.rearrange("p k (j t) -> p k j t", t=T),
                        zr[:, 4 * i - 8:4 * i - 4, :, 0:NCH].rearrange("p k t j -> p k j t"))
            dst = xsm[:, 8 * i - 32:8 * i - 24, lo * NS:lo * NS + NS]
            if i == 4:
                return dst, mixO[:, :, :]
            return (dst.rearrange("p k (b t) -> p k b t", t=T), zr[:, :, :, NCH:NJ].rearrange("p k t b -> p k b t"))

        def mix_high(e, parts):
            for i in parts:
                dst, src = mix_part(i, 0)
                nc.scalar.activation(dst, src, ACT.Copy).then_inc(S("mix_hi"), 1)

        def mix_low(e, eng, parts, done):
            for i in parts:
                e.wait_ge(S("mix_hi"), B("mix_hi") + i + 1)
                dst, src = mix_part(i, 1)
                eng.tensor_tensor(dst, src, mix_part(i, 0)[0].bitcast(F32), ALU.subtract).then_inc(S(done), 1)

        def mix_ready(e):
            e.wait_ge(S("mix_lo"), B("mix_lo") + 3)
            e.wait_ge(S("mix_lo_v"), B("mix_lo_v") + 3)

        def f_act(e):
            d_done(e)
            mix_high(e, (4, 5))

            def split(g):
                split_act(e, g, g, False, None)

            def evac_o(ch):
                _, c, g0, ng, n = ch
                e.wait_ge(S("w_used"), g0 + ng)
                if n == 0:
                    mix_ready(e)
                nc.scalar.activation(yt[0:NS, NT, n * CW:n * CW + CW], ps[bank(4, c)][64:128, :],
                                     ACT.Copy).then_inc(S("half"), 1)

            stream(e, split, WO, evac_o)
            for t in range(TILES):
                norm_act(e, "a", t, 1)
                norm_act(e, "a", t, 2)
                for i, (tt, _) in enumerate(GROUPS):
                    if tt == t:
                        turn_act(e, "a", i, 1)
            e.wait_ge(S("a_turn"), 2 * NGR)

            def evac_f(ch):
                kind, c, g0, ng, x = ch
                e.wait_ge(S("w_used"), g0 + ng)
                if kind == "down":
                    e.wait_ge(S("csm_used"), c - 12)
                    nc.scalar.activation(csm[:, :], ps[bank(4, c)][64:128, :], ACT.Copy).then_inc(S("half"), 1)
                    return
                f = x
                if f:
                    e.wait_ge(S("csm_used"), c - 12)
                def relu(t):
                    e.wait_ge(S(f"acc{t}"), c + 1)
                    if f:
                        e.wait_ge(S("r_lo"), B("r_lo") + 4 * (f - 1) + t + 1)
                    nc.scalar.activation(rv[t][:, :], ps[bank(t, c)][:, :], ACT.Relu).then_inc(S(f"out{t}"), 1)

                def high(t):
                    e.wait_ge(S("r_sq"), B("r_sq") + 4 * f + t + 1)
                    nc.scalar.activation(rhi[:, t, :], rv[t][:, :], ACT.Copy).then_inc(S("r_hi"), 1)

                relu(0)
                nc.scalar.activation(csm[:, :], ps[bank(4, c)][64:128, :], ACT.Copy).then_inc(S("half"), 1)
                relu(1)
                high(0)
                relu(2)
                high(1)
                relu(3)
                high(2)
                high(3)
                e.wait_ge(S("rs_T"), f + 1)
                nc.scalar.activation(rsm[:, :, 0:NS], ps[bank(4, c)][:, 0:4 * NS].rearrange("p (k n) -> p k n", k=4),
                                     ACT.Copy).then_inc(S("rs_hi"), 1)

            stream(e, split, FN, evac_f)
            for t in range(TILES):
                norm_act(e, "a", t, 3)

        def f_pe(e):
            d_done(e)
            e.wait_ge(S("mix_hi"), B("mix_hi") + 6)
            mix_ready(e)

            def free(e, t, c=0):
                e.wait_ge(S("csum" if t == 4 else f"out{t}"), c - 1 if t < 3 else c)

            for _, c, g0, ng, n in WO:
                pe_chunk(e, c, g0, g0, "x", KC, xhi, xlo, xsm, lambda e, t, c=c: free(e, t, c))
            for t in range(NT):
                e.wait_ge(S(f"out{t}"), 12)
            e.wait_ge(S("csum"), 12)
            for t in range(TILES):
                turn_pe(e, "a", xn2[t % 2], t, 1)
            e.wait_ge(S("a_lo"), 2 * NGR)
            e.wait_ge(S("a_val"), 2 * NGR)
            for kind, c, g0, ng, x in FN:
                if kind == "up":
                    pe_chunk(e, c, g0, g0, "w", KC, xhi, xlo, xsm, lambda e, t, c=c: free(e, t, c))
                    f = x
                    e.wait_ge(S("rs_sum"), f + 1)
                    for b in range(4):
                        mm = nc.tensor.transpose(ps[bank(4, c)][:, b * NS:b * NS + NS], csm[:, b * P:b * P + P],
                                                 ident[0:NS, 0:NS])
                    mm.then_inc(S("rs_T"), 1)
                else:
                    def need(k, t, f=x[0]):
                        if t == 0:
                            e.wait_ge(S("r_lo"), B("r_lo") + 4 * f + k + 1)
                        elif k == 0:
                            e.wait_ge(S("rs_lo"), f + 1)

                    pe_chunk(e, c, g0, g0, "x", 4, rhi, rlo, rsm, lambda e, t, c=c: free(e, t, c), None,
                             need if x[1] == 0 else None)

        def f_dve(e):
            own = owns["dve"]
            V = nc.vector
            d_done(e)

            mix_low(e, nc.vector, (0, 1, 4), "mix_lo_v")

            def split(g):
                split_dve(e, g, g)

            def evac_o(ch):
                _, c, g0, ng, n = ch
                cs = slice(n * CW, n * CW + CW)
                e.wait_ge(S(f"row_in{n % 2}"), 112 * (n // 2) + 112)
                mix_ready(e)
                for t in (3, 4, 0, 1, 2):
                    y = yt[0:tile_rows(t), t, cs]
                    g = gr[n % 2][t // 4][0:tile_rows(t), :]
                    if t == 4:
                        e.wait_ge(S("half"), c + 1)
                        V.tensor_tensor(y, y, ps[bank(4, c)][0:NS, :], ALU.add).then_inc(S("csum"), 1)
                        e.wait_ge(S("csum"), c + 1)
                        own(V.tensor_tensor(y, y, g, ALU.mult))
                    else:
                        e.wait_ge(S(f"acc{t}"), c + 1)
                        V.tensor_tensor(y, ps[bank(t, c)][:, :], g, ALU.mult).then_inc(S(f"out{t}"), 1)
                        e.wait_ge(S(f"out{t}"), c + 1)
                    own(V.scalar_tensor_tensor(y, xr[n % 2][t][0:tile_rows(t), :], ALPHA, y, ALU.mult, ALU.add))
                    ins = V.bn_stats(stats5[0:tile_rows(t), t, n, :], y)
                ins.then_inc(S("o_row"), 1)

            stream(e, split, WO, evac_o)
            e.wait_ge(S("gb_in"), 32)
            for t in range(TILES):
                r = tile_rows(t)
                y = yt[0:r, t, :]
                own(norm_dve(e, own, "a", y, t, lambda: e.wait_ge(S("o_row"), 4), 1, None, stats5[0:r, t, :, :]))
                own(V.tensor_tensor(y, y, grow[0:r, :], ALU.mult))
                V.tensor_tensor(y, y, brow[0:r, :], ALU.add).then_inc(S("x1"), 1)

                def ready():
                    e.wait_ge(S("x1"), B("x1") + t + 1)
                    if t >= 2:
                        e.wait_ge(S("a_turn"), NGR + 4 * (t - 1))
                norm_dve(e, own, "a", y, t, ready, 2, xn2[t % 2][0:r, :]).then_inc(S("a_xn"), 1)
                turn_dve(e, own, "a", t, 3, 1)
            e.wait_ge(S("x1_out"), 16 * TILES)
            e.wait_ge(S("a_turn"), 2 * NGR)

            def evac_f(ch):
                kind, c, g0, ng, x = ch
                if kind == "up":
                    f = x

                    def square(t):
                        e.wait_ge(S(f"out{t}"), c + 1)
                        nc.vector.tensor_tensor(rv[t][:, :], rv[t][:, :], rv[t][:, :], ALU.mult).then_inc(S("r_sq"), 1)

                    square(0)
                    e.wait_ge(S("half"), c + 1)
                    own(V.tensor_tensor(csm[:, :], csm[:, :], ps[bank(4, c)][0:NS, :], ALU.add))
                    V.scalar_tensor_tensor(csm[:, :], csm[:, :], 0.0, csm[:, :], ALU.max, ALU.mult).then_inc(
                        S("rs_sum"), 1)
                    for t in (1, 2, 3):
                        square(t)
                    e.wait_ge(S("rs_hi"), f + 1)
                    V.tensor_tensor(rsm[:, :, NS:], ps[bank(4, c)][:, 0:4 * NS].rearrange("p (k n) -> p k n", k=4),
                                    rsm[:, :, 0:NS].bitcast(F32), ALU.subtract).then_inc(S("rs_lo"), 1)
                    e.wait_ge(S("rs_lo"), f + 1)
                    V.tensor_copy(soft[:, 0:1], mv[:, 0:1]).then_inc(S("csum"), 1)
                    V.tensor_copy(soft[:, 1:2], mv[:, 0:1]).then_inc(S("csm_used"), 1)
                    return
                e.wait_ge(S("half"), c + 1)
                f, n = x
                cs = slice(n * CW, n * CW + CW)
                for t in (3, 4, 0, 1, 2):
                    y = yt[0:tile_rows(t), t, cs]
                    src = ps[bank(t, c)][0:tile_rows(t), :]
                    if f:
                        e.wait_ge(S("y_acc2"), B("y_acc2") + 4 * (f - 1) + n + 1)
                    if t < 4:
                        e.wait_ge(S(f"acc{t}"), c + 1)
                    if f == 0:
                        ins = V.tensor_copy(y, src)
                    else:
                        ins = V.tensor_tensor(y, y, src, ALU.add)
                    if t < 4:
                        ins.then_inc(S(f"out{t}"), 1)
                    else:
                        ins.then_inc(S("csum"), 1)
                        e.wait_ge(S("csum"), c + 1)
                        V.tensor_tensor(y, y, csm[:, :], ALU.add).then_inc(S("csm_used"), 1)
                if f == NF - 1:
                    e.wait_ge(S("last_in"), 16 * (4 + TILES))
                    for t in range(TILES):
                        y = yt[0:tile_rows(t), t, cs]
                        if t == 0:
                            e.wait_ge(S("csm_used"), c - 11)
                            e.wait_ge(S("out2"), c + 1)
                        own(V.tensor_tensor(y, y, g2row[t // 4][0:tile_rows(t), cs], ALU.mult))
                        own(V.scalar_tensor_tensor(y, x1t[t][0:tile_rows(t), cs], ALPHA, y, ALU.mult, ALU.add))
                        ins = V.bn_stats(stats5[0:tile_rows(t), t, n, :], y)
                    own(ins)
                V.tensor_copy(soft[:, 2:3], mv[:, 0:1]).then_inc(S("y_acc2"), 1)

            stream(e, split, FN, evac_f)
            e.wait_ge(S("y_acc2"), B("y_acc2") + 4 * NF)
            for t in range(TILES):
                r = tile_rows(t)
                y = yt[0:r, t, :]
                own(norm_dve(e, own, "a", y, t, lambda: None, 3, None, stats5[0:r, t, :, :]))
                V.tensor_tensor(y, y, grow2[0:r, :], ALU.mult).then_inc(S("y_row"), 1)

        @block.sync
        def _(e):
            e.dma_start(crow[0:1, :], a["c_prompt"]).then_inc(S("c_in"), 16)
            e.dma_start(crow[1:1 + NB, :], a["c_sample"]).then_inc(S("c_in"), 16)
            e.dma_start(badar[:, :], a["b_ada"].rearrange("o (k p) -> (o k) p", p=P)).then_inc(S("bada_in"), 16)
            bias_in(e, 0)
            e.dma_start(bf[:, :], a["b_f"].rearrange("o h -> h o")).then_inc(S("bf_in"), 16)
            for n in range(ADA1):
                for q in range(NGC):
                    g = n * NGC + q
                    if g >= 6:
                        e.wait_ge(S("ada_used"), g - 5)
                    e.dma_start((raw + adr)[g % 6][:, :, :],
                                wada[q * GK * P:(q + 1) * GK * P, n * CW:n * CW + CW].rearrange(
                                    "(k p) n -> p k n", p=P)).then_inc(S(ADA_FULL[g % 6]), 16)
            e.wait_ge(S("ada_used"), ADA1 * NGC)

            def load_p(g):
                col, q = PJ[g // NGC][1], g % NGC
                load_w(e, g, g, win[q * GK * P:(q + 1) * GK * P, col:col + CW], g < NR)

            for g in range(3):
                load_p(g)
            for x in range(NGP):
                for g in (2 * x, 2 * x + 1):
                    if g >= 3:
                        e.wait_ge(S("ada_used"), ADA1 * NGC + g - 2)
                    n, q = ADA1 + g // NGC, g % NGC
                    e.dma_start(adr[g % 3][:, :, :],
                                wada[q * GK * P:(q + 1) * GK * P, n * CW:n * CW + CW].rearrange(
                                    "(k p) n -> p k n", p=P)).then_inc(S(f"adb_full{g % 3}"), 16)
                if x + 3 < NGP:
                    load_p(x + 3)
                if x >= 4 and ada_events(x - 4):
                    gate_dma(e, ada_events(x - 4))
            for x in range(NGP - 4, NGP):
                if ada_events(x):
                    gate_dma(e, ada_events(x))
            for ev in ADA_END:
                gate_dma(e, ev)
            p_sp(e)
            s_sp(e)
            d_sp(e)
            f_sp(e)

        @block.gpsimd
        def _(e):
            own = owns["pool"] = Own(e, S("pool_own"))
            own(nc.gpsimd.memset(ident[:, :], 1.0))
            own(nc.gpsimd.affine_select(out=ident[:, :], in_=ident[:, :], compare_op=ALU.is_equal, fill=0.0,
                                        base=0, pattern=[[-1, P]], channel_multiplier=1))
            own(nc.gpsimd.memset(diag[:, :], 0.0))
            own(nc.gpsimd.affine_select(out=diag[:, :], in_=diag[:, :], compare_op=ALU.is_ge, fill=NEG,
                                        base=0, pattern=[[-1, P]], channel_multiplier=1))
            own(nc.gpsimd.memset(later[:, :], 1.0))
            lv = later[:, :].rearrange("p (b j) -> p b j", b=NB)
            own(nc.gpsimd.affine_select(out=lv, in_=lv, compare_op=ALU.is_ge, fill=0.0, base=0,
                                        pattern=[[-PAGES, NB], [-1, PAGES]], channel_multiplier=1))
            own(nc.gpsimd.affine_select(out=lv, in_=lv, compare_op=ALU.is_ge, fill=0.0, base=PAGES - 1,
                                        pattern=[[PAGES, NB], [0, PAGES]], channel_multiplier=-1))
            own(nc.gpsimd.memset(m8[:, :], 1.0))
            own(nc.gpsimd.affine_select(out=m8[:, :], in_=m8[:, :], compare_op=ALU.is_ge, fill=0.0, base=0,
                                        pattern=[[-GC, T]], channel_multiplier=1))
            own(nc.gpsimd.affine_select(out=m8[:, :], in_=m8[:, :], compare_op=ALU.is_ge, fill=0.0, base=GC - 1,
                                        pattern=[[GC, T]], channel_multiplier=-1))
            iv = ident[:, :].rearrange("p (j i) -> p j i", j=4)
            own(nc.gpsimd.memset(ones[:, :], 1.0))
            own(nc.gpsimd.tensor_copy(scT[:, 0, 0:9], iv[:, 0, 0:9]))
            for j in range(1, 4):
                own(nc.gpsimd.tensor_tensor(scT[:, 0, 0:9], scT[:, 0, 0:9], iv[:, j, 0:9], ALU.add))
            own(nc.gpsimd.tensor_copy(selp[:, :], scT[:, 0, 0:1].to_broadcast([P, P])))
            own(nc.gpsimd.tensor_copy(sels[:, :].rearrange("p (b q) -> p b q", b=NB),
                                      scT[:, 0, 1:9].unsqueeze(2).to_broadcast([P, NB, NQ])))
            own(nc.gpsimd.memset(scT[:, :, :], 0.0))
            own(nc.gpsimd.memset(keep[:, :], 1.0))
            nc.gpsimd.memset(keep[:, 0:1], 0.0)
            nc.gpsimd.memset(keep[:, SEQ:SEQ + NS].rearrange("p (b q) -> p b q", q=NQ)[:, :, 0:1],
                             0.0).then_inc(S("consts"), 1)

            def load_x(t):
                if t >= 2:
                    e.wait_ge(S("a_turn"), 4 * (t - 1))
                src = x_p[t * P:t * P + P, :] if t < NT else x_s
                e.dma_start(xrow[t % 2][0:tile_rows(t), :], src).then_inc(S(f"x_in{t % 2}"), 16)

            load_x(0)
            load_x(1)
            for i, (t, q) in enumerate(GROUPS):
                turn_pool(e, "a", i)
                if q == 3 and t + 2 < TILES:
                    load_x(t + 2)
            e.dma_start(wfr[:, :, :], win[:, 3 * AW:3 * AW + H].rearrange("(k p) h -> p k h", p=P)).then_inc(
                S("wf_in"), 16)
            nc.gpsimd.memset(wfh[:, :, :].bitcast(F32), 0.0)
            own(nc.gpsimd.memset(wfl[:, :, :].bitcast(F32), 0.0))
            e.wait_ge(S("wf_in"), 16)
            own(nc.gpsimd.tensor_copy(wfh[:, :, 0:H], wfr[:, :, :]))
            nc.gpsimd.tensor_tensor(wfl[:, :, 0:H], wfr[:, :, :], wfh[:, :, 0:H].bitcast(F32),
                                    ALU.subtract).then_inc(S("wf"), 1)
            for c, (kind, col, half) in enumerate(PJ):
                hs = slice(half * CW, half * CW + CW)
                e.wait_ge(S("csum"), c + 1)
                dst = {"q": qs_d, "u": us_d, "k": o["k_sample"][0].rearrange("b q h d -> (b q) (h d)"),
                       "v": o["v_sample"][0].rearrange("b q h d -> (b q) (h d)")}[kind]
                e.dma_start(dst[:, hs], csum[c % 2][:, :]).then_inc(S(f"csum_out{c % 2}"), 16)
                if kind == "u":
                    for t in range(NT):
                        e.wait_ge(S(f"out{t}"), c + 1)
                        r0 = half * CW + t * P
                        e.dma_start(u_d[r0:r0 + P, :, 0:NCH], ust[:, t, :, :]).then_inc(S("ust_out"), 16)
                if kind == "v" and half == 1:
                    for t in range(NT):
                        e.wait_ge(S(f"out{t}"), c + 1)
                        e.dma_start(o["v_prompt"][0, 0, t * P:t * P + P].rearrange("s h d -> s (h d)"),
                                    vtok[:, t, :]).then_inc(S("v_out"), 16)
            e.wait_ge(S("v_out"), 64)
            e.wait_ge(S("ust_out"), 128)
            e.wait_ge(S("csum_out0"), 64)
            e.wait_ge(S("csum_out1"), 64)
            p_pool(e)
            s_pool(e)
            d_pool(e)
            f_pool(e)

        def evac(c, t, eng, kind, half):
            src = ps[bank(t, c)]
            if kind in "qk":
                dst = (qT if kind == "q" else kT)[:, half * 4 + t, :]
            elif kind == "u":
                dst = ust[:, t, :, :]
                src = src[:, :].rearrange("p (j s) -> p s j", s=T)
            else:
                dst = vtok[:, t, half * CW:half * CW + CW]
            if kind != "u":
                src = src[:, :]
            if kind == "q":
                ins = (nc.scalar.mul(dst, src, SCALE) if eng == "a"
                       else nc.vector.tensor_scalar(dst, src, SCALE, None, ALU.mult))
            else:
                ins = (nc.scalar.activation(dst, src, ACT.Copy) if eng == "a" else nc.vector.tensor_copy(dst, src))
            ins.then_inc(S(f"out{t}"), 1)

        @block.scalar
        def _(e):
            e.wait_ge(S("c_in"), 32)
            nc.scalar.activation(crow[:, :], crow[:, :], ACT.Silu).then_inc(S("silu"), 1)
            norm_act(e, "a", 0)
            norm_act(e, "a", 1)
            for n in range(ADA1):
                e.wait_ge(S("ada_used"), NGC * (n + 1))
                if n >= 2:
                    e.wait_ge(S("ada_t"), n - 1)
                nc.scalar.activation(gpart[n % 2][:, :], ps[n % 2][:, :], ACT.Copy).then_inc(S("ada_g"), 1)
            for t in range(TILES):
                if t >= 2:
                    norm_act(e, "a", t)
                for i, (tt, _) in enumerate(GROUPS):
                    if tt == t:
                        turn_act(e, "a", i)
            own = Own(e, S("act_own"))
            e.wait_ge(S("lg"), 1)
            own(nc.scalar.activation(fcum[:, :], logf[:, :], ACT.Abs))
            nc.scalar.activation(fcum[:, :], fcum[:, :], ACT.Exp, scale=-1.0).then_inc(S("lf_e"), 1)
            e.wait_ge(S("lf_w"), 1)
            nc.scalar.activation(lf2[:, :], lf1[:, :], ACT.Ln).then_inc(S("lf_l"), 1)
            NGT = len(PJ) * NGC
            e.wait_ge(S("fcum"), 1)
            for g in range(NGT + LAG):
                if g >= 6 and (g - 6) % 4 == 0:
                    n = ADA1 + (g - 6) // 4
                    e.wait_ge(S("ada_used"), NGC * (n + 1))
                    nc.scalar.activation(gpart[n % 2][:, :], ps[5 + n % 2][:, :], ACT.Copy).then_inc(S("ada_g"), 1)
                if g >= NGC + LAG - 1 and (g - LAG + 1) % NGC == 0:
                    c = (g - LAG + 1) // NGC - 1
                    kind, _, half = PJ[c]
                    e.wait_ge(S("w_used"), NGC * (c + 1))
                    if c >= 2:
                        e.wait_ge(S(f"csum_out{c % 2}"), 16 * (c // 2))
                    nc.scalar.activation(csum[c % 2][:, :], ps[bank(4, c)][64:128, :], ACT.Copy).then_inc(S("half"), 1)
                    if kind == "u" and half == 1:
                        e.wait_ge(S("ust_out"), 64)
                    for t in (3, 1):
                        evac(c, t, "a", kind, half)
                if g < NGT:
                    split_act(e, g, g, g < NW, None)
            p_act(e)
            s_act(e)
            d_act(e)
            f_act(e)

        @block.tensor
        def _(e):
            e.wait_ge(S("consts"), 1)
            e.wait_ge(S("silu"), 1)
            for k in range(KC):
                mm = nc.tensor.transpose(ps[6][:, k * 16:k * 16 + 9], crow[:, k * P:k * P + P], ident[0:9, 0:9])
            e.wait_ge(S("bada_in"), 16)
            mm = nc.tensor.transpose(ps[7][:, 0:96], badar[:, :], ident[0:96, 0:96])
            mm.then_inc(S("c_turn"), 1)
            e.wait_ge(S("scT"), 1)

            def ada_turn(n):
                e.wait_ge(S("ada_g"), n + 1)
                if n >= 2:
                    e.wait_ge(S("ada_m"), n - 1)
                for b in range(4):
                    mm = nc.tensor.transpose(ps[2 + n % 2][:, b * P:b * P + P], gpart[n % 2][:, b * P:b * P + P],
                                             ident[:, :])
                mm.then_inc(S("ada_t"), 1)

            for n in range(ADA1):
                if n >= 2:
                    e.wait_ge(S("ada_g"), n - 1)
                for q in range(NGC):
                    g = n * NGC + q
                    e.wait_ge(S(ADA_FULL[g % 6]), 16 * (g // 6) + 16)
                    for k2 in range(GK):
                        k = q * GK + k2
                        j = k % 4
                        mm = nc.tensor.matmul(ps[n % 2][32 * j:32 * j + 32, :], scT[:, k, :], (raw + adr)[g % 6][:, k2, :],
                                              start=k < 4, stop=k >= KC - 4)
                    mm.then_inc(S("ada_used"), 1)
                if n >= 1:
                    ada_turn(n - 1)
            ada_turn(ADA1 - 1)
            for t in range(TILES):
                turn_pe(e, "a", xrow[t % 2], t)
            e.wait_ge(S("a_lo"), NGR)
            e.wait_ge(S("wf"), 1)
            for k in range(KC):
                st, en = k == 0, k == KC - 1
                nc.tensor.matmul(ps[2][:, :], wfh[:, k, :], xhi[:, k, :], start=st, stop=False)
                nc.tensor.matmul(ps[2][:, :], wfh[:, k, :], xlo[:, k, :], start=False, stop=False)
                nc.tensor.matmul(ps[2][:, :], wfl[:, k, :], xhi[:, k, :], start=False, stop=en)
                nc.tensor.matmul(ps[3][:, 0:2 * NS], wfh[:, k, :], xsm[:, k, :], start=st, stop=False)
                mm = nc.tensor.matmul(ps[3][:, 0:2 * NS], wfl[:, k, :], xsm[:, k, :], start=False, stop=en)
            mm.then_inc(S("f_acc"), 1)
            e.wait_ge(S("lg"), 1)

            for c, (kind, _, _) in enumerate(PJ):
                def free(e, t, c=c):
                    if c:
                        e.wait_ge(S("csum" if t == 4 else f"out{t}"), c)
                pe_chunk(e, c, c * NGC, c * NGC, "x" if kind == "v" else "w", KC, xhi, xlo, xsm, free,
                         lambda x: ada_slot(e, x))
            for ev in ADA_END:
                ada_event_pe(e, ev)
            p_pe(e)
            s_pe(e)
            d_pe(e)
            f_pe(e)

        @block.vector
        def _(e):
            own = owns["dve"] = Own(e, S("dve_own"))
            e.wait_ge(S("consts"), 1)
            e.wait_ge(S("c_turn"), 1)
            own(nc.vector.tensor_copy(badaT[:, :], ps[7][:, 0:96]))
            own(nc.vector.tensor_scalar(badaT[:, KC:2 * KC], ps[7][:, KC:2 * KC], 1.0, None, ALU.add))
            nc.vector.tensor_scalar(badaT[:, 4 * KC:5 * KC], ps[7][:, 4 * KC:5 * KC], 1.0, None, ALU.add)
            nc.vector.tensor_copy(scT[:, :, 0:9], ps[6][:, 0:KC * 16].rearrange("p (k i) -> p k i", k=KC)[:, :, 0:9]
                                  ).then_inc(S("scT"), 1)
            e.wait_ge(S("scT"), 1)
            def first_norm(t):
                norm_dve(e, own, "a", xrow[t % 2], t,
                         lambda: e.wait_ge(S(f"x_in{t % 2}"), 16 * (t // 2) + 16)).then_inc(S("a_xn"), 1)

            first_norm(0)
            first_norm(1)
            for n in range(ADA1):
                e.wait_ge(S("ada_t"), n + 1)
                m4 = modT[:, 4 * n:4 * n + 4, :]
                own(nc.vector.tensor_reduce(
                    m4, ps[2 + n % 2][:, :].rearrange("p (b j i) -> p b i j", b=4, j=4)[:, :, 0:9, :], AX.X, ALU.add))
                nc.vector.tensor_tensor(m4, m4, badaT[:, 4 * n:4 * n + 4].unsqueeze(2).to_broadcast([P, 4, 9]),
                                        ALU.add).then_inc(S("ada_m"), 1)
            e.wait_ge(S("ada_m"), ADA1)
            for t in range(TILES):
                if t >= 2:
                    first_norm(t)
                turn_dve(e, own, "a", t, 0)
            e.wait_ge(S("f_acc"), 1)
            e.wait_ge(S("bf_in"), 16)
            own(nc.vector.tensor_scalar(logf[:, 0:SEQ], ps[2][0:H, :], bf[:, 0:1], None, ALU.add))
            own(nc.vector.tensor_scalar(logf[:, SEQ:], ps[3][0:H, 0:NS], bf[:, 0:1], None, ALU.add))
            nc.vector.tensor_tensor(logf[:, SEQ:], logf[:, SEQ:], ps[3][0:H, NS:2 * NS], ALU.add).then_inc(S("lg"), 1)
            own(nc.vector.tensor_copy(lf3[:, 0:1], logf[:, 0:1]))
            e.wait_ge(S("lf_e"), 1)
            nc.vector.tensor_scalar(lf1[:, :], fcum[:, :], 1.0, None, ALU.add).then_inc(S("lf_w"), 1)
            e.wait_ge(S("lf_w"), 1)
            own(nc.vector.scalar_tensor_tensor(lf3[:, :], lf1[:, :], -1.0, fcum[:, :], ALU.add, ALU.subtract))
            e.wait_ge(S("lf_l"), 1)
            own(nc.vector.reciprocal(fcum[:, :], lf1[:, :]))
            own(nc.vector.tensor_tensor(lf3[:, :], lf3[:, :], fcum[:, :], ALU.mult))
            own(nc.vector.tensor_tensor(lf3[:, :], lf2[:, :], lf3[:, :], ALU.subtract))
            own(nc.vector.scalar_tensor_tensor(logf[:, :], logf[:, :], 0.0, lf3[:, :], ALU.min, ALU.subtract))
            own(nc.vector.tensor_tensor_scan(fcum[:, :], keep[:, :], logf[:, :], 0.0, ALU.mult, ALU.add))
            nc.vector.tensor_scalar(nfc[:, :], fcum[:, :], -1.0, None, ALU.mult).then_inc(S("fcum"), 1)
            NGT = len(PJ) * NGC
            for g in range(NGT + LAG):
                if g >= 3 and g - 3 < NGP and ada_events(g - 3):
                    ada_evac(e, own, ada_events(g - 3))
                if g >= NGC + LAG - 1 and (g - LAG + 1) % NGC == 0:
                    c = (g - LAG + 1) // NGC - 1
                    kind, _, half = PJ[c]
                    e.wait_ge(S("half"), c + 1)
                    nc.vector.tensor_tensor(csum[c % 2][:, :], csum[c % 2][:, :], ps[bank(4, c)][0:64, :],
                                            ALU.add).then_inc(S("csum"), 1)
                    if kind == "u" and half == 1:
                        e.wait_ge(S("ust_out"), 64)
                    for t in (0, 2):
                        e.wait_ge(S(f"acc{t}"), c + 1)
                        evac(c, t, "v", kind, half)
                if g < NGT:
                    split_dve(e, g, g)
            for ev in ADA_END:
                ada_evac(e, own, ev)
            p_dve(e)
            s_dve(e)
            d_dve(e)
            f_dve(e)


_OUT_SHAPES = [("y_prompt", (1, SEQ, D)), ("y_sample", (NB, NQ, D)),
               ("k_prompt", (1, 1, SEQ, H, DH)), ("v_prompt", (1, 1, SEQ, H, DH)), ("logf_prompt", (1, 1, SEQ, H)),
               ("ssm_re_prompt", (1, 1, G, NST)), ("ssm_im_prompt", (1, 1, G, NST)),
               ("k_sample", (1, NB, NQ, H, DH)), ("v_sample", (1, NB, NQ, H, DH)), ("logf_sample", (1, NB, NQ, H)),
               ("ssm_re_sample", (1, NB, G, NST)), ("ssm_im_sample", (1, NB, G, NST))]


def kernel(**inputs):
    import numpy as np
    import concourse.bacc as bacc
    from concourse.bass_utils import run_bass_kernel_spmd

    nc = bacc.Bacc("TRN2", target_bir_lowering=False, num_devices=1)
    arrays, ins, outs = {}, {}, {}
    for name, x in inputs.items():
        x = np.ascontiguousarray(x)
        arrays[f"in_{name}"] = x
        ins[name] = nc.dram_tensor(f"in_{name}", x.shape, mybir.dt.from_np(x.dtype), kind="ExternalInput").ap()
    for name, shape in _OUT_SHAPES:
        outs[name] = nc.dram_tensor(f"out_{name}", shape, F32, kind="ExternalOutput").ap()
    program(nc, ins, outs)
    r = run_bass_kernel_spmd(nc, [arrays], core_ids=[0])
    return tuple(r.results[0][f"out_{name}"] for name, _ in _OUT_SHAPES)
```
